# Optimizing a Trainium2 kernel written in Bass

```python
import jax, jax.numpy as jnp
from jax import lax
import numpy as np

D_MODEL = 2048
BATCH = 1
SEQ = 512
DEPTH = 1
DEC_BATCH = 8
DEC_SEQ = 1
PAST_LEN = 2048
PAGE_SIZE = 128

HEAD_DIM = 128
N_HEADS = D_MODEL // HEAD_DIM
N_KV_HEADS = 4
KV_GROUP = N_HEADS // N_KV_HEADS
ATT_WIDTH = N_HEADS * HEAD_DIM
KV_WIDTH = N_KV_HEADS * HEAD_DIM
IDX_HEADS = 16
IDX_DIM = 128
IDX_SCALE = (IDX_HEADS * IDX_DIM) ** -0.5
TOPK_MAX = 256
Q_BLOCK = 128
POOL_WINDOWS = (2, 4, 8, 16)
POOL_GROUPS = 4
POOL_WIDTH = D_MODEL // 2
POOL_GROUP_DIM = POOL_WIDTH // POOL_GROUPS
POOL_STATE = max(POOL_WINDOWS) - 1
ROPE_THETA = 10000.0
EPS = 1e-6
IN_SIZES = (ATT_WIDTH, KV_WIDTH, KV_WIDTH, IDX_HEADS * IDX_DIM, IDX_DIM, IDX_HEADS,
            ATT_WIDTH, POOL_WIDTH, POOL_WIDTH, D_MODEL, D_MODEL)
IN_WIDTH = sum(IN_SIZES)

kernel_name = 'dsa_pool_gated_hybrid_step'

def _rms(x, g):
    xf = x.astype(jnp.float32)
    y = xf * lax.rsqrt(jnp.mean(xf * xf, axis=-1, keepdims=True) + EPS)
    return (y * g.astype(jnp.float32)).astype(x.dtype)

def _rope(x, pos):
    half = x.shape[-1] // 2
    inv = ROPE_THETA ** (-jnp.arange(half, dtype=jnp.float32) / half)
    ang = pos.astype(jnp.float32)[:, None] * inv[None, :]
    cos = jnp.cos(ang)[:, None, :]
    sin = jnp.sin(ang)[:, None, :]
    xf = x.astype(jnp.float32)
    x1, x2 = xf[..., :half], xf[..., half:]
    return jnp.concatenate([x1 * cos - x2 * sin, x2 * cos + x1 * sin], axis=-1).astype(x.dtype)

def _modulate(x, c, g_norm, w_ada, b_ada):
    mod = c @ w_ada + b_ada
    shift, scale, gate = jnp.split(mod, 3, axis=-1)
    h = _rms(x, g_norm) * (1 + scale[:, None, :]) + shift[:, None, :]
    return h, gate

def _project_in(h, w_in, pos):
    z = h @ w_in
    parts = []
    off = 0
    for n in IN_SIZES:
        parts.append(z[..., off:off + n])
        off += n
    q, k, v, qi, ki, wi, ga, u, gb, ma, mb = parts
    b, t = h.shape[:2]
    q = _rope(q.reshape(b, t, N_HEADS, HEAD_DIM), pos)
    k = _rope(k.reshape(b, t, N_KV_HEADS, HEAD_DIM), pos)
    v = v.reshape(b, t, N_KV_HEADS, HEAD_DIM)
    qi = _rope(qi.reshape(b, t, IDX_HEADS, IDX_DIM), pos)
    ki = _rope(ki.reshape(b, t, 1, IDX_DIM), pos)[:, :, 0]
    wi = wi * IDX_SCALE
    return q, k, v, qi, ki, wi, ga, u, gb, ma, mb

def _indexer_topk(qi, wi, ki, q_pos, topk):
    s = jnp.einsum('bqhd,bsd->bqhs', qi, ki, preferred_element_type=jnp.float32)
    score = jnp.einsum('bqh,bqhs->bqs', wi.astype(jnp.float32), jax.nn.relu(s))
    k_pos = jnp.arange(ki.shape[1], dtype=jnp.int32)
    causal = k_pos[None, :] <= q_pos[:, None]
    score = jnp.where(causal[None], score, -jnp.inf)
    _, idx = lax.top_k(score, topk)
    valid = idx <= q_pos[None, :, None]
    return idx, valid

def _take_rows(rows, idx):
    return jax.vmap(lambda r, i: r[i])(rows, idx)

def _paged_rows(cache, page_table, new_rows, idx):
    past_len = page_table.shape[1] * PAGE_SIZE
    flat = cache.reshape((-1,) + cache.shape[2:])
    pidx = jnp.minimum(idx, past_len - 1)
    page = jax.vmap(lambda pt, i: pt[i])(page_table, pidx // PAGE_SIZE)
    past = flat[page * PAGE_SIZE + pidx % PAGE_SIZE].astype(new_rows.dtype)
    nidx = jnp.clip(idx - past_len, 0, new_rows.shape[1] - 1)
    new = _take_rows(new_rows, nidx)
    is_past = (idx < past_len).reshape(idx.shape + (1,) * (new.ndim - idx.ndim))
    return jnp.where(is_past, past, new)

def _gathered_attention(q, k_sel, v_sel, valid):
    b, t = q.shape[:2]
    qg = q.reshape(b, t, N_KV_HEADS, KV_GROUP, HEAD_DIM)
    logits = jnp.einsum('btngd,btjnd->btngj', qg, k_sel,
                        preferred_element_type=jnp.float32) * (HEAD_DIM ** -0.5)
    logits = jnp.where(valid[:, :, None, None, :], logits, -jnp.inf)
    p = jax.nn.softmax(logits, axis=-1).astype(v_sel.dtype)
    o = jnp.einsum('btngj,btjnd->btngd', p, v_sel)
    return o.reshape(b, t, ATT_WIDTH)

def _prompt_attention(q, k, v, qi, ki, wi):
    b, s = q.shape[:2]
    topk = min(TOPK_MAX, s // 4)
    nblk = s // Q_BLOCK

    def blocks(a):
        return a.reshape((b, nblk, Q_BLOCK) + a.shape[2:]).swapaxes(0, 1)

    pos = jnp.arange(s, dtype=jnp.int32).reshape(nblk, Q_BLOCK)

    def one_block(args):
        qb, qib, wib, pb = args
        idx, valid = _indexer_topk(qib, wib, ki, pb, topk)
        return _gathered_attention(qb, _take_rows(k, idx), _take_rows(v, idx), valid)

    o = lax.map(one_block, (blocks(q), blocks(qi), blocks(wi), pos))
    return o.swapaxes(0, 1).reshape(b, s, ATT_WIDTH)

def _sample_attention(q, k, v, qi, ki, wi, cache_k, cache_v, cache_kidx, page_table):
    b, t = q.shape[:2]
    past = page_table.shape[1] * PAGE_SIZE
    topk = min(TOPK_MAX, (past + t) // 4)
    ki_past = cache_kidx[page_table].reshape(b, past, IDX_DIM).astype(ki.dtype)
    ki_all = jnp.concatenate([ki_past, ki], axis=1)
    q_pos = past + jnp.arange(t, dtype=jnp.int32)
    idx, valid = _indexer_topk(qi, wi, ki_all, q_pos, topk)
    k_sel = _paged_rows(cache_k, page_table, k, idx)
    v_sel = _paged_rows(cache_v, page_table, v, idx)
    return _gathered_attention(q, k_sel, v_sel, valid)

def _pool_mixer(u, prev, pos0, w_pool, s_pool):
    b, t, c = u.shape
    ext = jnp.concatenate([prev.astype(u.dtype), u], axis=1)
    cs = jnp.cumsum(ext.astype(jnp.float32), axis=1)
    cs = jnp.concatenate([jnp.zeros((b, 1, c), jnp.float32), cs], axis=1)
    end = cs[:, POOL_STATE + 1:]
    n_avail = pos0 + jnp.arange(t, dtype=jnp.int32) + 1
    means = []
    for g, w in enumerate(POOL_WINDOWS):
        lo, hi = g * POOL_GROUP_DIM, (g + 1) * POOL_GROUP_DIM
        start = cs[:, POOL_STATE + 1 - w:POOL_STATE + 1 - w + t, lo:hi]
        cnt = jnp.minimum(n_avail, w).astype(jnp.float32)[None, :, None]
        means.append((end[..., lo:hi] - start) / cnt)
    pooled = (jnp.concatenate(means, axis=-1) - u.astype(jnp.float32)).astype(u.dtype)
    mixed = jnp.einsum('btgc,gcd->btgd', pooled.reshape(b, t, POOL_GROUPS, POOL_GROUP_DIM), w_pool)
    return mixed.reshape(b, t, c) * s_pool, ext[:, -POOL_STATE:]

def _merge(x, attn, pool, ga, gb, ma, mb, gate, w_a_proj, w_b_proj, w_out):
    a = (attn * jax.nn.silu(ga)) @ w_a_proj
    bb = (pool * jax.nn.silu(gb)) @ w_b_proj
    m = jax.nn.sigmoid(ma) * a + jax.nn.sigmoid(mb) * bb
    return x + gate[:, None, :] * (m @ w_out)

def setup_inputs(seed: int = 0) -> dict:
    key = jax.random.key(seed)
    ks = jax.random.split(key, 20)
    f = jnp.float32
    n_pages = PAST_LEN // PAGE_SIZE
    n_used = DEC_BATCH * n_pages
    n_pool = n_used + max(n_used // 4, 1)

    def nrm(k, shape, s):
        return jax.random.normal(k, shape, f) * s

    page_table = jax.random.permutation(ks[8], n_pool)[:n_used].reshape(DEC_BATCH, n_pages).astype(jnp.int32)
    return {
        'x_prompt': nrm(ks[0], (BATCH, SEQ, D_MODEL), 1.0),
        'x_sample': nrm(ks[1], (DEC_BATCH, DEC_SEQ, D_MODEL), 1.0),
        'c_prompt': nrm(ks[2], (BATCH, D_MODEL), 1.0),
        'c_sample': nrm(ks[3], (DEC_BATCH, D_MODEL), 1.0),
        'cache_k': nrm(ks[4], (DEPTH, n_pool, PAGE_SIZE, N_KV_HEADS, HEAD_DIM), 1.0),
        'cache_v': nrm(ks[5], (DEPTH, n_pool, PAGE_SIZE, N_KV_HEADS, HEAD_DIM), 1.0),
        'cache_kidx': nrm(ks[6], (DEPTH, n_pool, PAGE_SIZE, IDX_DIM), 1.0),
        'state_pool': nrm(ks[7], (DEPTH, DEC_BATCH, POOL_STATE, POOL_WIDTH), 1.0),
        'page_table': page_table,
        'g_norm': 1.0 + nrm(ks[9], (DEPTH, D_MODEL), 0.01),
        'w_ada': nrm(ks[10], (DEPTH, D_MODEL, 3 * D_MODEL), 0.5 * D_MODEL ** -0.5),
        'b_ada': nrm(ks[11], (DEPTH, 3 * D_MODEL), 0.01),
        'w_in': nrm(ks[12], (DEPTH, D_MODEL, IN_WIDTH), D_MODEL ** -0.5),
        'w_pool': nrm(ks[13], (DEPTH, POOL_GROUPS, POOL_GROUP_DIM, POOL_GROUP_DIM), POOL_GROUP_DIM ** -0.5),
        's_pool': 1.0 + nrm(ks[14], (DEPTH, POOL_WIDTH), 0.1),
        'w_a_proj': nrm(ks[15], (DEPTH, ATT_WIDTH, D_MODEL), ATT_WIDTH ** -0.5),
        'w_b_proj': nrm(ks[16], (DEPTH, POOL_WIDTH, D_MODEL), POOL_WIDTH ** -0.5),
        'w_out': nrm(ks[17], (DEPTH, D_MODEL, D_MODEL), D_MODEL ** -0.5),
        'g_final': 1.0 + nrm(ks[18], (D_MODEL,), 0.01),
    }

def reference(x_prompt, x_sample, c_prompt, c_sample, cache_k, cache_v, cache_kidx, state_pool,
              page_table, g_norm, w_ada, b_ada, w_in, w_pool, s_pool, w_a_proj, w_b_proj, w_out, g_final):
    bp, sp = x_prompt.shape[:2]
    ds = x_sample.shape[1]
    past = page_table.shape[1] * PAGE_SIZE
    pos_p = jnp.arange(sp, dtype=jnp.int32)
    pos_s = past + jnp.arange(ds, dtype=jnp.int32)
    xp, xs = x_prompt, x_sample
    kp_l, vp_l, kip_l, pp_l = [], [], [], []
    ks_l, vs_l, kis_l, ps_l = [], [], [], []
    for l in range(DEPTH):
        h, gate = _modulate(xp, c_prompt, g_norm[l], w_ada[l], b_ada[l])
        q, k, v, qi, ki, wi, ga, u, gb, ma, mb = _project_in(h, w_in[l], pos_p)
        attn = _prompt_attention(q, k, v, qi, ki, wi)
        prev0 = jnp.zeros((bp, POOL_STATE, POOL_WIDTH), u.dtype)
        pool, pst = _pool_mixer(u, prev0, 0, w_pool[l], s_pool[l])
        xp = _merge(xp, attn, pool, ga, gb, ma, mb, gate, w_a_proj[l], w_b_proj[l], w_out[l])
        kp_l.append(k); vp_l.append(v); kip_l.append(ki); pp_l.append(pst)
        h, gate = _modulate(xs, c_sample, g_norm[l], w_ada[l], b_ada[l])
        q, k, v, qi, ki, wi, ga, u, gb, ma, mb = _project_in(h, w_in[l], pos_s)
        attn = _sample_attention(q, k, v, qi, ki, wi, cache_k[l], cache_v[l], cache_kidx[l], page_table)
        pool, sst = _pool_mixer(u, state_pool[l], past, w_pool[l], s_pool[l])
        xs = _merge(xs, attn, pool, ga, gb, ma, mb, gate, w_a_proj[l], w_b_proj[l], w_out[l])
        ks_l.append(k); vs_l.append(v); kis_l.append(ki); ps_l.append(sst)
    y_prompt = _rms(xp, g_final)
    y_sample = _rms(xs, g_final)
    return (y_prompt, y_sample,
            jnp.stack(kp_l), jnp.stack(vp_l), jnp.stack(kip_l), jnp.stack(pp_l),
            jnp.stack(ks_l), jnp.stack(vs_l), jnp.stack(kis_l), jnp.stack(ps_l))


_drawn_inputs = setup_inputs


def setup_inputs(seed=0):
    import zlib

    import numpy as np

    out = dict(_drawn_inputs(seed))
    spreads = {}
    factors = {'g_norm': 5.916, 'b_ada': 4.969, 'g_final': 5.658}
    for name, (base, spread) in spreads.items():
        noise = np.random.default_rng([zlib.crc32(name.encode()), seed]).standard_normal(out[name].shape)
        drawn = base * np.exp(spread * noise) if base else spread * noise
        out[name] = __import__('jax').numpy.asarray(drawn.astype(out[name].dtype))
    for name, factor in factors.items():
        out[name] = (out[name] * factor).astype(out[name].dtype)
    return out
```

```python
from contextlib import ExitStack

import numpy as np
import concourse.bass as bass
import concourse.mybir as mybir

F32 = mybir.dt.float32
F32R = mybir.dt.float32r
BF16 = mybir.dt.bfloat16
U32 = mybir.dt.uint32
I32 = mybir.dt.int32
ALU = mybir.AluOpType
ACT = mybir.ActivationFunctionType
AX = mybir.AxisListType

P = 128
D = 2048
KT = D // P
SEQ = 512
NB = 8
TOK = SEQ + NB
HALF = TOK // 2
HEADS = 16
KVH = 4
PAST = 2048
PAGES = PAST // P
TOPK_P = 128
TOPK_S = 256
PW = 1024
WINDOWS = (2, 4, 8, 16)
STATE = 15
EPS = 1e-6
ATT_SCALE = P ** -0.5
IDX_SCALE = (HEADS * P) ** -0.5
MASKED = -1e30
TAKEN = -3e38
C_Q, C_K, C_V, C_QI, C_KI, C_WI = 0, 2048, 2560, 3072, 5120, 5248
C_GA, C_U, C_GB, C_MA, C_MB = 5264, 7312, 8336, 9360, 11408
Q_ADA, Q_A, Q_GATE, Q_B, Q_C, Q_D, Q_E, Q_F1, Q_F2, Q_G, Q_END = 0, 16, 25, 33, 37, 53, 61, 77, 85, 93, 101
N_A, N_GATE, N_B, N_C, N_D, N_E, N_F1, N_F2, N_G = 4, 13, 13, 15, 31, 39, 55, 63, 71
OFF = [0, 128, 384, 768, 1280]
S_AT = [(0, 0), (1, 0), (0, 128), (2, 0)]
PT_AT = {(qb, kb): sum(4 - k for k in range(kb)) + qb - kb for kb in range(4) for qb in range(kb, 4)}


class Chain:

    def __init__(self, eng, sem):
        self.eng, self.sem, self.base, self.k, self.per = eng, sem, 0, 0, None

    def count(self, ins):
        ins.then_inc(self.sem, 1)
        self.k += 1

    def step(self, ins):
        self.count(ins)
        self.eng.wait_ge(self.sem, self.at + self.k)

    at = 0

    def enter(self, i, first, per):
        self.base += self.k
        self.at = self.base + (i - first) * per
        self.k, self.per = 0, per

    def leave(self, times):
        assert self.k == self.per, (self.k, self.per)
        self.base += times * self.per
        self.at, self.k = self.base, 0


def build(nc, t, out):
    ctx = ExitStack()
    sem_of = {}

    def sem(name):
        if name not in sem_of:
            sem_of[name] = ctx.enter_context(nc.semaphore(name))
        return sem_of[name]

    BASE = 16512

    def at(name, off, shape, dt=F32):
        size = int(np.prod(shape[1:])) * (2 if dt == BF16 else 4)
        assert off + size <= 229368 - BASE, (name, off, size)
        return nc.alloc_sbuf_tensor_at(name, shape, dt, offset=BASE + off)

    act_hi = at("act_hi", 0, [P, KT, TOK], F32R)
    act_lo = at("act_lo", 33280, [P, KT, TOK], F32R)
    square_dump = at("square_dump", 33280, [P, D])
    raw = [at(f"raw{p}", 66560 + 8192 * p, [P, 2048]) for p in range(2)]
    whi = [at(f"whi{p}", 82944 + 8192 * p, [P, 2048], F32R) for p in range(2)]
    wlo = [at(f"wlo{p}", 99328 + 8192 * p, [P, 2048], F32R) for p in range(2)]
    A0 = 115712
    ident = at("ident", A0, [P, P])
    identb = at("identb", A0 + 512, [P, P], BF16)
    misc = at("misc", A0 + 768, [P, 512])
    qSm = at("qSm", A0 + 2816, [P, NB, KVH, HEADS])
    qiS = at("qiS", A0 + 4864, [P, NB, HEADS])
    sgaS = at("sgaS", A0 + 5376, [P, HEADS, NB])
    attS = at("attS", A0 + 5888, [P, HEADS, NB])
    A1 = A0 + 6400
    xs = at("xs", A1, [NB, D])
    scoreS = at("scoreS", A1, [NB, PAST + 8])
    ys = at("ys", A1, [NB, D])
    A2 = A1 + 8256
    TAIL = A2 + 78336
    cst = at("cst", A2, [P, KT, P], F32R)
    x_tok = at("x_tok", A2 + 8192, [P, 4, D])
    H = at("H", A2 + 40960, [P, KT, TOK])
    modb = [at(f"modb{c}", A2 + 74240 + 2048 * c, [18, 512]) for c in range(2)]
    mA = at("mA", TAIL, [P, KT, 9])
    mB = at("mB", TAIL + 576, [P, KT, 9])
    tri = at("tri", TAIL + 1152, [P, P])
    rows_cs = at("rows_cs", TAIL + 1664, [P, P])
    rows_cp = at("rows_cp", TAIL + 2176, [16, P])
    rows_b = at("rows_b", TAIL + 2688, [48, P])
    rows_gs = at("rows_gs", TAIL + 3200, [24, P])
    A3 = A2 + 128
    cosT = at("cosT", A3 + 8192, [P, TOK])
    sinT = at("sinT", A3 + 10272, [P, TOK])
    kiT = at("kiT", A3 + 12352, [P, TOK])
    accS = at("accS", A3 + 14432, [P, 1280])
    reluP = at("reluP", A3 + 19552, [P, 1280])
    qiT = [at(f"qiT{p}", A3 + 24672 + 2080 * p, [P, TOK]) for p in range(2)]
    swp = at("swp", A3 + 28832, [P, TOK])
    ebuf = at("ebuf", A3 + 30912, [P, TOK])
    wiT = at("wiT", A3 + 32992, [HEADS, TOK])
    gate_rows = at("gate_rows", A3 + 35072, [NB + 1, D])
    gate_bias = at("gate_bias", A3 + 43264, [NB + 1, D])
    kT = at("kT", A2, [P, KVH, TOK])
    vtok = at("vtok", A3 + 35072, [P, 4, 512])
    maskb = at("maskb", A3 + 43264, [P, 1280], BF16)
    BG = A3 + 45824
    silu_ga = at("silu_ga", BG, [P, HEADS, TOK])
    ktok = at("ktok", A3 + 52224, [P, 4, 512])
    stok = at("stok", A3 + 60416, [NB, 2, 512])
    vT = [at(f"vT{p}", A3 + 64512 + 2080 * p, [P, TOK]) for p in range(2)]
    kib = at("kib", BG, [P, PAGES, P])
    kiTb = at("kiTb", BG + 8192, [P, PAST + 8])
    reluS = at("reluS", BG + 16448, [HEADS, PAST + 8])
    wiD = at("wiD", BG + 24704, [HEADS, NB, NB])
    kitok = at("kitok", A3 + 68672, [P, 4, P])
    kistok = at("kistok", A3 + 70720, [NB, P])
    prob = accS
    probT = reluP
    qT = qiT[0]
    vcur = at("vcur", A3 + 26752, [P, 4, P])
    pool_hi = at("pool_hi", A2, [P, 8, TOK], F32R)
    pool_lo = at("pool_lo", A2 + 16640, [P, 8, TOK], F32R)
    big1 = at("big1", A2, [P, KT, TOK])
    big2 = at("big2", A2 + 33280, [P, KT, TOK])
    Z0 = A2 + 33280
    wpool = at("wpool", Z0, [P, 4, 2, 256])
    state = at("state", Z0 + 8192, [NB * STATE, PW])
    ub = [at(f"ub{p}", Z0 + 12288 + 2112 * p, [P, 16 + SEQ]) for p in range(2)]
    ext = [at(f"ext{p}", Z0 + 16512 + 512 * p, [P, NB, 16]) for p in range(2)]
    win = [at(f"win{p}", Z0 + 17536 + 2112 * p, [P, 16 + SEQ]) for p in range(2)]
    pooled = at("pooled", Z0 + 21760, [P, 2, TOK])
    pstage = at("pstage", Z0 + 25920, [STATE, 256])
    sstage = at("sstage", Z0 + 26944, [NB, 256])
    wsum8 = at("wsum8", Z0 + 27968, [P, NB])
    Z = A2 + 66560
    e_back = at("e_back", Z, [P, TOK])
    s_back = at("s_back", Z + 2080, [P, TOK])
    idxS = at("idxS", Z + 4160, [NB, TOPK_S], U32)
    idx8 = at("idx8", Z + 5184, [NB, 8], U32)
    ksel = at("ksel", A2, [P, 2, 512])
    vsel = at("vsel", A2 + 4096, [P, 2, 512])
    kselT = at("kselT", A2 + 8192, [P, KVH, 256])
    pS = at("pS", A2 + 12288, [HEADS, 256])
    pST = at("pST", A2 + 13312, [P, 2, HEADS])
    rowf = at("rowf", A2 + 13440, [NB, 6, 256])
    rowT = at("rowT", A2 + 19584, [P, 2, NB], U32)
    ptf = at("ptf", A2 + 19648, [NB, PAGES])
    pti = at("pti", A2 + 19712, [NB, PAGES], I32)
    att_stage = [at(f"att_stage{s}", Z + 2048 * s, [P, SEQ]) for s in range(4)]
    yrow = at("yrow", A2, [P, 4, D])
    sm = at("sm", Z, [P, KT, P], F32R)
    gate_p = at("gate_p", A2 + 33280, [P, D])
    gate_s = at("gate_s", A2 + 41472, [NB, D])
    gfin = at("gfin", A2 + 49664, [P, D])
    xch = at("xch", A2 + 57856, [P, 4, 512])
    srow = at("srow", A0 + 2816, [2 * NB, 512])

    bT = misc[:, 0:48]
    gT = misc[:, 48:64]
    spT = misc[:, 64:72]
    ss = misc[:, 72:80]
    rstd = misc[:, 80:88]
    mxq = misc[:, 88:92]
    nmq = misc[:, 92:96]
    sumq = misc[:, 96:100]
    rq = misc[:, 100:104]
    wiq = misc[:, 104:152]
    rcnt = misc[:, 152:216]
    sel9 = misc[0:18, 404:413]
    sel8 = misc[0:16, 414:478]
    cT = misc[:, 240:384].rearrange("p (t b) -> p t b", b=9)
    max8 = misc[:, 392:400]
    eps = misc[:, 400:401]

    acc = [ctx.enter_context(nc.psum_tensor(f"acc{p}", [P, 2, 512], F32)) for p in range(2)]
    ps = ctx.enter_context(nc.psum_tensor("ps", [P, 4, 512], F32))
    accv = [a[:, :, 0:HALF] for a in acc]
    modT = acc[0][:, 1, 0:288].rearrange("p (t b) -> p t b", b=9)
    xsT = acc[1][:, 1, 0:128].rearrange("p (t b) -> p t b", b=NB)

    att_dram = nc.dram_tensor("att_dram", (HEADS, P, SEQ), F32).ap()
    gate_dram = nc.dram_tensor("gate_dram", (NB + 1, D), F32).ap()

    raw_landed = [sem(f"raw_landed{p}") for p in range(2)]
    hi_ready = [sem(f"hi_ready{p}") for p in range(2)]
    lo_ready = [sem(f"lo_ready{p}") for p in range(2)]
    unit_done = [sem(f"unit_done{p}") for p in range(2)]
    acc_free = [sem(f"acc_free{p}") for p in range(2)]
    S = sem

    w_in, w_ada, w_a, w_b, w_out = (t[n][0] for n in ("w_in", "w_ada", "w_a_proj", "w_b_proj", "w_out"))

    def cols(w, c):
        return w[:, bass.ds(c, P)].rearrange("(k p) n -> p k n", p=P)

    def quarter(w, kq, c):
        return w[kq * 512:(kq + 1) * 512, bass.ds(c, 512)].rearrange("(k p) n -> p k n", p=P)

    def halves(ap):
        return ap.rearrange("p (a n) -> p a n", a=2)

    block = ctx.enter_context(nc.Block())

    @block.sync
    def _(sp):
        def load(q, p, src, first=False):
            if not first:
                sp.wait_ge(lo_ready[p], q)
            k, n = src.shape[1], src.shape[2]
            dst = raw[p][:, 0:k * n].rearrange("p (k n) -> p k n", n=n)
            sp.dma_start(dst, src).then_inc(raw_landed[p], 16)

        for dst, src in ((rows_cs[:], t["c_sample"].rearrange("b (t p) -> (b t) p", p=P)),
                         (rows_cp[:], t["c_prompt"].rearrange("b (t p) -> (b t) p", p=P)),
                         (rows_b[:], t["b_ada"].rearrange("b (t p) -> (b t) p", p=P)),
                         (rows_gs[0:16, :], t["g_norm"].rearrange("b (t p) -> (b t) p", p=P)),
                         (rows_gs[16:24, :], t["s_pool"].rearrange("b (t p) -> (b t) p", p=P)),
                         (ident[:], t["k_ident"]), (misc[0:18, 404:478], t["k_sel"]),
                         (rcnt, t["k_rcnt"]), (tri[:], t["k_tri"])):
            sp.dma_start(dst, src).then_inc(S("tables_landed"), 16)
        for u in range(32):
            load(u // 2, u % 2, quarter(w_ada, u % 4, 512 * (u // 4)), first=u < 2)
            if u == 1:
                sp.dma_start(xs[:], t["x_sample"].rearrange("b s d -> (b s) d")).then_inc(S("xs_landed"), 16)
            if 2 <= u < 6:
                i = u - 2
                sp.dma_start(x_tok[:, i, :], t["x_prompt"][0, i * P:(i + 1) * P, :]).then_inc(S(f"x_landed{i}"), 16)
        load(Q_A, 0, cols(w_in, C_WI))
        load(Q_A, 1, cols(w_in, C_KI))
        sp.wait_ge(S("xT_act"), 4)
        sp.dma_start(cosT[:], t["k_cos"]).then_inc(S("rope_landed"), 16)
        sp.dma_start(sinT[:], t["k_sin"]).then_inc(S("rope_landed"), 16)
        with sp.Fori(0, 8) as i:
            load(Q_A + 1 + i, 0, cols(w_in, C_QI + 256 * i))
            load(Q_A + 1 + i, 1, cols(w_in, C_QI + P + 256 * i))
        sp.wait_ge(S("act_lo_ready"), KT)
        sp.dma_start(gate_bias[:], t["b_ada"][0:1, 2 * D:3 * D].broadcast_to([NB + 1, D])
                     ).then_inc(S("gate_bias_landed"), 16)
        for c in range(4):
            for kq in range(4):
                load(Q_GATE + 2 * c + kq // 2, kq % 2, quarter(w_ada, kq, 2 * D + 512 * c))
        for j in range(8):
            load(Q_B + j // 2, j % 2, cols(w_in, C_K + P * j))
            if j == 3:
                sp.wait_ge(S("gate_rows_ready"), 4)
                sp.dma_start(gate_dram, gate_rows[:]).then_inc(S("gate_stored"), 16)
        sp.wait_ge(S("ki_tok_ready"), 1)
        sp.dma_start(out["kidx_p"].rearrange("(t p) d -> p t d", p=P), kitok[:]).then_inc(S("out_front"), 16)
        sp.dma_start(out["kidx_s"], kistok[:]).then_inc(S("out_front"), 16)
        load(Q_C, 0, cols(w_in, C_Q))
        load(Q_C, 1, cols(w_in, C_GA))
        sp.wait_ge(S("kv_evac"), 8)
        sp.dma_start(out["k_p"].rearrange("(t p) d -> p t d", p=P), ktok[:]).then_inc(S("out_front"), 16)
        sp.dma_start(out["v_p"].rearrange("(t p) d -> p t d", p=P), vtok[:]).then_inc(S("out_front"), 16)
        sp.dma_start(out["k_s"], stok[:, 0, :]).then_inc(S("out_front"), 16)
        sp.dma_start(out["v_s"], stok[:, 1, :]).then_inc(S("out_front"), 16)
        sp.wait_ge(S("out_front"), 6 * 16)
        for b in range(NB):
            if b:
                sp.wait_ge(S("si_T"), b)
            for pg in range(PAGES):
                page = sp.value_load(t["page_table"][b:b + 1, pg:pg + 1], min_val=0, max_val=t["n_pool"] - 1)
                sp.dma_start(kib[:, pg, :], t["cache_kidx"][0, bass.ds(page, 1)].rearrange("o s d -> (o s) d")
                             ).then_inc(S("kib_landed"), 16)
        with sp.Fori(1, HEADS) as h:
            load(Q_C + h, 0, cols(w_in, C_Q + P * h))
            load(Q_C + h, 1, cols(w_in, C_GA + P * h))
        load(Q_D, 0, cols(w_in, C_U))
        load(Q_D, 1, cols(w_in, C_U + P))
        sp.wait_ge(S("att_stored"), HEADS * 16)
        sp.wait_ge(S("front_done"), 1)
        sp.dma_start(wpool[:], t["w_pool"][0].rearrange("g (c p) d -> p g c d", p=P)).then_inc(S("pool_landed"), 16)
        sp.dma_start(state[:], t["state_pool"][0].rearrange("b s c -> (b s) c")).then_inc(S("pool_landed"), 16)
        sp.dma_start(out["pool_s"][:, 0:STATE - 1, :], t["state_pool"][0, :, 1:STATE, :]).then_inc(S("out_pool"), 16)
        for g in range(4):
            if g:
                load(Q_D + 2 * g, 0, cols(w_in, C_U + 256 * g))
                load(Q_D + 2 * g, 1, cols(w_in, C_U + 256 * g + P))
            load(Q_D + 2 * g + 1, 0, cols(w_in, C_GB + 256 * g))
            load(Q_D + 2 * g + 1, 1, cols(w_in, C_GB + 256 * g + P))
            sp.wait_ge(S("u_tok_ready"), 2 * g + 2)
            sp.dma_start(out["pool_p"][:, 256 * g:256 * g + 256], pstage[:]).then_inc(S("out_pool"), 16)
            sp.dma_start(out["pool_s"][:, STATE - 1, 256 * g:256 * g + 256], sstage[:]).then_inc(S("out_pool"), 16)
        sp.wait_ge(S("out_pool"), 9 * 16)
        with sp.Fori(Q_E, Q_F1) as q:
            load(q, 0, cols(w_in, P * q + (C_MB - P * Q_E)))
            load(q, 1, cols(w_b, P * q - P * Q_E))
        load(Q_F1, 0, cols(w_in, C_MA))
        load(Q_F1, 1, cols(w_in, C_MA + P))
        sp.wait_ge(unit_done[1], Q_F1)
        sp.dma_start(pti[:], t["page_table"]).then_inc(S("pt_landed"), 16)
        for b in range(NB):
            if b:
                sp.wait_ge(S("sa_pv"), b)
            for dst, src in ((ksel, out["k_s"]), (vsel, out["v_s"])):
                for hf in range(2):
                    sp.dma_start(dst[:, hf, :], src[b:b + 1, :].broadcast_to([P, 512])).then_inc(S("sa_new"), 16)
        with sp.Fori(1, 8) as i:
            load(Q_F1 + i, 0, cols(w_in, C_MA + 256 * i))
            load(Q_F1 + i, 1, cols(w_in, C_MA + 256 * i + P))
        load(Q_F2, 0, cols(w_a, 0))
        load(Q_F2, 1, cols(w_a, P))
        sp.wait_ge(S("sma_ready"), 16)
        for k in range(KT):
            if k >= 4:
                sp.wait_ge(S("att_split"), k - 3)
            sp.dma_start(att_stage[k % 4][:], att_dram[k]).then_inc(S(f"att_landed{k % 4}"), 16)
        with sp.Fori(1, 8) as i:
            load(Q_F2 + i, 0, cols(w_a, 256 * i))
            load(Q_F2 + i, 1, cols(w_a, 256 * i + P))
        sp.dma_start(ys[:], t["x_sample"].rearrange("b s d -> (b s) d")).then_inc(S("xs2_landed"), 16)
        for kq in range(2):
            load(Q_G, kq, quarter(w_out, kq, 0))
        sp.wait_ge(S("sm_ready"), 1)
        sp.dma_start(gate_p[:], gate_dram[0:1, :].broadcast_to([P, D])).then_inc(S("g_landed"), 16)
        sp.dma_start(gate_s[:], gate_dram[1:NB + 1, :]).then_inc(S("g_landed"), 16)
        sp.dma_start(gfin[:], t["g_final"].rearrange("(o d) -> o d", o=1).broadcast_to([P, D])
                     ).then_inc(S("g_landed"), 16)
        sp.dma_start(xch[:], t["x_prompt"][0, :, 0:512].rearrange("(t p) n -> p t n", p=P)
                     ).then_inc(S("xch_landed"), 16)
        for kq in range(2, 4):
            load(Q_G + 1, kq - 2, quarter(w_out, kq, 0))
        with sp.Fori(1, 4) as c:
            for kq in range(4):
                load(Q_G + 2 * c + kq // 2, kq % 2, quarter(w_out, kq, 512 * c))
            sp.wait_ge(S("y_added"), 4 * c)
            sp.dma_start(xch[:], t["x_prompt"][0, :, bass.ds(512 * c, 512)].rearrange("(t p) n -> p t n", p=P)
                         ).then_inc(S("xch_landed"), 16)
        for i in range(4):
            sp.wait_ge(S("y_ready"), i + 1)
            sp.dma_start(out["y_p"][i * P:(i + 1) * P, :], yrow[:, i, :]).then_inc(S("out_y"), 16)
        sp.wait_ge(S("y_ready"), 5)
        sp.dma_start(out["y_s"], ys[:]).then_inc(S("out_y"), 16)
        sp.wait_ge(S("out_y"), 5 * 16)

    @block.gpsimd
    def _(pool):
        def lo(q, p):
            pool.wait_ge(hi_ready[p], q + 1)
            nc.gpsimd.tensor_tensor(wlo[p][:], raw[p][:], whi[p][:].bitcast(F32), ALU.subtract).then_inc(lo_ready[p], 1)

        with pool.Fori(Q_ADA, Q_A) as q:
            lo(q, 0)
        with pool.Fori(Q_A, Q_GATE) as q:
            lo(q, 0)
            lo(q, 1)
        with pool.Fori(Q_GATE, Q_B) as q:
            lo(q, 0)
        with pool.Fori(Q_B, Q_C) as q:
            lo(q, 0)
            lo(q, 1)
        with pool.Fori(0, HEADS) as h:
            lo(Q_C + h, 0)
            lo(Q_C + h, 1)
            pool.wait_ge(S("kv_evac"), 8)
            pool.wait_ge(S("attn_pv"), h)
            nc.gpsimd.tensor_copy(vcur[:], vtok[:, :, bass.ds((h // 4) * P, P)]).then_inc(S("vcur_ready"), 1)
        with pool.Fori(Q_D, Q_F1) as q:
            lo(q, 0)
            lo(q, 1)
        lo(Q_F1, 0)
        lo(Q_F1, 1)
        kf = t["cache_k"][0].rearrange("n s h d -> (n s) (h d)")
        vf = t["cache_v"][0].rearrange("n s h d -> (n s) (h d)")
        pool.wait_ge(S("rows_ready"), 1)
        for b in range(NB):
            pool.wait_ge(S("sa_new"), 64 * (b + 1))
            for hf in range(2):
                for dst, src in ((ksel, kf), (vsel, vf)):
                    nc.gpsimd.indirect_dma_start(
                        dst[:, hf, :], None, src, bass.IndirectOffsetOnAxis(ap=rowT[:, hf, b:b + 1], axis=0),
                        bounds_check=src.shape[0] - 1, oob_is_err=False).then_inc(S("sa_sel"), 16)
        with pool.Fori(Q_F1 + 1, Q_G) as q:
            lo(q, 0)
            lo(q, 1)
        with pool.Fori(Q_G, Q_END) as q:
            lo(q, 0)

    @block.scalar
    def _(act):
        def hi(q, p, first=False):
            act.wait_ge(raw_landed[p], 16 * (q + 1))
            if not first:
                act.wait_ge(unit_done[p], q)
            nc.scalar.copy(whi[p][:], raw[p][:]).then_inc(hi_ready[p], 1)

        def root(n, i, summed, count):
            act.wait_ge(summed, count)
            nc.scalar.activation(rstd[0:n, i:i + 1], ss[0:n, i:i + 1], ACT.Sqrt, bias=eps[0:n, :],
                                 scale=1.0 / D).then_inc(S("root_ready"), 1)

        hi(0, 0, first=True)
        hi(0, 1, first=True)
        act.wait_ge(S("tables_landed"), 9 * 16)
        nc.scalar.copy(identb[:], ident[:]).then_inc(S("identb_ready"), 1)
        act.wait_ge(S("cT_ready"), 1)
        act.wait_ge(S("cst_zero"), 1)
        nc.scalar.copy(cst[:, :, 0:9], cT).then_inc(S("cst_hi"), 1)
        act.wait_ge(S("xs_landed"), 16)
        nc.scalar.activation(square_dump[0:NB, :], xs[:], ACT.Square, accum_out=ss[0:NB, 4:5]).then_inc(S("ss_ready"), 1)
        root(NB, 4, S("ss_ready"), 1)

        def mod_rows(n):
            act.wait_ge(unit_done[1], 2 * n + 2)
            if n >= 2:
                act.wait_ge(S("mod_mm"), n - 1)
            nc.scalar.copy(modb[n % 2][:], acc[n % 2][0:18, 0, :]).then_inc(acc_free[n % 2], 1)

        for q in range(Q_ADA, Q_A):
            hi(q + 1, 0)
            if q % 2 == 0 and q:
                mod_rows(q // 2 - 1)
            hi(q + 1, 1)
            if q in (1, 2, 3, 5):
                i = (1, 2, 3, 5).index(q)
                act.wait_ge(S(f"x_landed{i}"), 16)
                act.wait_ge(S("ss_ready"), i + 1)
                nc.scalar.activation(square_dump[:], x_tok[:, i, :], ACT.Square,
                                     accum_out=ss[:, i:i + 1]).then_inc(S("ss_ready"), 1)
                root(P, i, S("ss_ready"), i + 2)
            if q in (4, 6, 8, 10):
                i = (q - 4) // 2
                act.wait_ge(S("xT_done"), i + 1)
                for j in range(2):
                    last = nc.scalar.copy(H[:, 4 * j:4 * j + 4, i * P:(i + 1) * P],
                                          ps[:, j, :].rearrange("p (k n) -> p k n", n=P))
                last.then_inc(S("xT_act"), 1)
        mod_rows(7)
        for k in range(KT):
            act.wait_ge(S("H_ready"), k + 1)
            nc.scalar.copy(act_hi[:, k, :], H[:, k, :]).then_inc(S("act_hi_ready"), 1)

        def relu_scores(h, first=False):
            act.wait_ge(S("idx_mm"), h + 1)
            if not first:
                act.wait_ge(S("idx_acc"), h)
            for b in (1, 2, 3):
                w = (b + 1) * P
                last = nc.scalar.activation(reluP[:, OFF[b]:OFF[b] + w], ps[:, b - 1, 0:w], ACT.Relu)
            last.then_inc(S("idx_relu"), 1)

        hi(Q_A + 1, 0)
        hi(Q_A + 1, 1)
        hi(Q_A + 2, 0)
        hi(Q_A + 2, 1)
        relu_scores(0, first=True)
        with act.Fori(1, 8) as i:
            hi(Q_A + 2 + i, 0)
            relu_scores(2 * i - 1)
            hi(Q_A + 2 + i, 1)
            relu_scores(2 * i)
        def gate_rows_part(c):
            act.wait_ge(unit_done[1], Q_GATE + 2 * c + 2)
            act.wait_ge(S("mod_mm"), 8)
            if c >= 2:
                act.wait_ge(S("gate_mm"), c - 1)
            nc.scalar.copy(modb[c % 2][:], acc[c % 2][0:18, 0, :]).then_inc(S("gate_part"), 1)

        for q in range(Q_GATE, Q_B):
            c = (q - Q_GATE) // 2
            hi(q + 1, 0)
            if q == Q_GATE + 1:
                relu_scores(15)
            if q % 2 == Q_GATE % 2 and c:
                gate_rows_part(c - 1)
            hi(q + 1, 1)
        gate_rows_part(3)
        for q in range(Q_B, Q_C):
            hi(q + 1, 0)
            hi(q + 1, 1)
        for b in range(NB):
            act.wait_ge(S("si_T"), b + 1)
            nc.scalar.copy(kiTb[:, 0:1024], ps[:, 0:2, :].rearrange("p a n -> p (a n)")).then_inc(S("si_ka"), 1)
            act.wait_ge(S("si_qk"), b + 1)
            nc.scalar.activation(reluS[:, 0:PAST], ps[0:HEADS, :, :].rearrange("p a n -> p (a n)"), ACT.Relu)
            nc.scalar.activation(reluS[:, PAST:PAST + 1], acc[0][0:HEADS, 0, 0:1], ACT.Relu).then_inc(S("si_relu"), 1)

        def body_c(h, first=False):
            q = Q_C + h
            hi(q + 1, 0)
            if not first:
                act.wait_ge(S("attn_T"), h)
                nc.scalar.copy(probT[:, 0:512], ps[:, 0, :]).then_inc(S("pt_act"), 1)
            hi(q + 1, 1)
            act.wait_ge(unit_done[1], q + 1)
            if not first:
                act.wait_ge(S("sga_ready"), h)
            nc.scalar.activation(halves(ebuf[:]), accv[1], ACT.Exp, scale=-1.0).then_inc(S("ega_ready"), 1)
            act.wait_ge(S("nm_ready"), h + 1)
            for b in range(4):
                bank, c = S_AT[b]
                w = (b + 1) * P
                last = nc.scalar.activation(prob[:, OFF[b]:OFF[b] + w], ps[:, bank, c:c + w], ACT.Exp,
                                            bias=nmq[:, b:b + 1], scale=ATT_SCALE, accum_out=sumq[:, b:b + 1])
            last.then_inc(S("exp_done"), 1)
            if not first:
                act.wait_ge(S("attn_evac"), h)
                act.dma_start(att_dram[bass.ds(h - 1, 1)].rearrange("o p n -> (o p) n"), silu_ga[:, h - 1, 0:SEQ]
                              ).then_inc(S("att_stored"), 16)

        body_c(0, first=True)
        with act.Fori(1, HEADS) as h:
            body_c(h)
        act.wait_ge(S("attn_T"), HEADS)
        nc.scalar.copy(probT[:, 0:512], ps[:, 0, :]).then_inc(S("pt_act"), 1)
        act.wait_ge(S("attn_evac"), HEADS)
        act.dma_start(att_dram[HEADS - 1], silu_ga[:, HEADS - 1, 0:SEQ]).then_inc(S("att_stored"), 16)
        act.wait_ge(S("att_stored"), HEADS * 16)
        act.wait_ge(S("front_done"), 1)
        for g in range(4):
            q = Q_D + 2 * g
            hi(q + 1, 0)
            hi(q + 1, 1)
            for j in range(2):
                hi(q + 2, j)
                if g or j:
                    act.wait_ge(S("pg_ready"), 2 * g + j)
                nc.scalar.activation(halves(e_back[:]), accv[j], ACT.Exp, scale=-1.0).then_inc(S("egb_ready"), 1)
                act.wait_ge(S("pg_ready"), 2 * g + j + 1)
                nc.scalar.copy(pool_hi[:, 2 * g + j, :], s_back[:]).then_inc(S("pool_hi_ready"), 1)
        act.wait_ge(S("pg_ready"), 8)
        with act.Fori(0, KT) as j:
            q = Q_E + j
            hi(q + 1, 0)
            act.wait_ge(S("smb_ready"), j)
            nc.scalar.activation(halves(e_back[:]), accv[0], ACT.Exp, scale=-1.0).then_inc(acc_free[0], 1)
            hi(q + 1, 1)
        act.wait_ge(S("smb_ready"), KT)
        for b in range(NB):
            act.wait_ge(S("sa_T"), b + 1)
            nc.scalar.copy(kselT[:, 0:2, :].rearrange("p a n -> p (a n)"), ps[:, 0, :]).then_inc(S("sa_ka"), 1)
            act.wait_ge(S("sa_nm"), b + 1)
            nc.scalar.activation(pS[:], ps[0:HEADS, 2, 0:256], ACT.Exp, bias=nmq[0:HEADS, 0:1], scale=ATT_SCALE,
                                 accum_out=sumq[0:HEADS, 0:1]).then_inc(S("sa_exp"), 1)
        with act.Fori(0, 8) as i:
            q = Q_F1 + i
            for p in range(2):
                hi(q + 1, p)
                act.wait_ge(S("sma_ready"), 2 * i + p)
                nc.scalar.activation(halves(e_back[:]), accv[p], ACT.Exp, scale=-1.0).then_inc(acc_free[p], 1)
        for k in range(KT):
            act.wait_ge(S(f"att_landed{k % 4}"), 16 * (k // 4 + 1))
            if k == 0:
                act.wait_ge(S("attS_ready"), NB)
            nc.scalar.copy(act_hi[:, k, 0:SEQ], att_stage[k % 4][:])
            nc.scalar.copy(act_hi[:, k, SEQ:TOK], attS[:, k, :]).then_inc(S("att_hi_ready"), 1)
        with act.Fori(Q_F2, Q_G) as q:
            hi(q + 1, 0)
            hi(q + 1, 1)
        for k in range(KT):
            act.wait_ge(S("m_ready"), k + 1)
            nc.scalar.copy(act_hi[:, k, :], big2[:, k, :]).then_inc(S("m_hi_ready"), 1)
        act.wait_ge(S("sm_zero"), 1)
        nc.scalar.copy(sm[:, :, 0:NB], big2[:, :, SEQ:TOK]).then_inc(S("sm_hi_ready"), 1)
        with act.Fori(Q_G, Q_END - 1) as q:
            hi(q + 1, 0)
            hi(q + 1, 1)
        for i in range(5):
            act.wait_ge(S("y_all"), 1)
            if i:
                act.wait_ge(S("ssy_ready"), i)
            src = yrow[:, i, :] if i < 4 else ys[:]
            n = P if i < 4 else NB
            nc.scalar.activation(xch[0:n].rearrange("p a n -> p (a n)"), src, ACT.Square,
                                 accum_out=ss[0:n, i:i + 1]).then_inc(S("ssy_ready"), 1)
            root(n, i, S("ssy_ready"), i + 1)

    @block.vector
    def _(dve):
        v = nc.vector
        chain = Chain(dve, sem("dve_chain"))
        step = chain.step

        def lo(q, p):
            dve.wait_ge(hi_ready[p], q + 1)
            v.tensor_tensor(wlo[p][:], raw[p][:], whi[p][:].bitcast(F32), ALU.subtract).then_inc(lo_ready[p], 1)

        def inverse_root(n, i, count):
            dve.wait_ge(S("root_ready"), count)
            step(v.reciprocal(rstd[0:n, i:i + 1], rstd[0:n, i:i + 1]))

        v.memset(eps, EPS)
        v.memset(cst[:].bitcast(F32), 0.0).then_inc(S("cst_zero"), 1)
        dve.wait_ge(S("rows_T"), 1)
        v.tensor_copy(cT[:, :, 1:9], ps[:, 0, 0:128].rearrange("p (b t) -> p t b", b=NB))
        v.tensor_copy(bT, ps[:, 1, 16:64])
        v.tensor_copy(misc[:, 48:72], ps[:, 1, 64:88])
        v.tensor_copy(cT[:, :, 0], ps[:, 1, 0:16]).then_inc(S("cT_ready"), 1)
        lo(0, 1)
        dve.wait_ge(S("cst_hi"), 1)
        v.tensor_tensor(cst[:, :, 9:18], cT, cst[:, :, 0:9].bitcast(F32), ALU.subtract).then_inc(S("cst_ready"), 1)
        inverse_root(NB, 4, 1)
        v.tensor_scalar(xs[:], xs[:], rstd[0:NB, 4:5], None, ALU.mult).then_inc(S("xs_ready"), 1)
        for q in range(1, Q_A):
            lo(q, 1)
            if q in (2, 3, 4, 6):
                i = (2, 3, 4, 6).index(q)
                inverse_root(P, i, i + 2)
                v.tensor_scalar(x_tok[:, i, :], x_tok[:, i, :], rstd[:, i:i + 1], None, ALU.mult
                                ).then_inc(S("xhat_ready"), 1)
            if q == 3:
                dve.wait_ge(S("xs_T"), 1)
                step(v.tensor_copy(H[:, :, SEQ:TOK], xsT))
            if q in (5, 7, 9, 11):
                i = (q - 5) // 2
                dve.wait_ge(S("xT_done"), i + 1)
                for j in range(2, 4):
                    last = v.tensor_copy(H[:, 4 * j:4 * j + 4, i * P:(i + 1) * P],
                                         ps[:, j, :].rearrange("p (k n) -> p k n", n=P))
                last.then_inc(S("xT_dve"), 1)
        dve.wait_ge(S("mod_mm"), 8)

        def per_tok(a):
            return a.unsqueeze(2).broadcast_to([P, KT, 9])

        v.tensor_tensor(mB[:], modT[:, 0:KT, :], per_tok(bT[:, 0:16]), ALU.add)
        step(v.tensor_tensor(mA[:], modT[:, KT:2 * KT, :], per_tok(bT[:, 16:32]), ALU.add))
        step(v.scalar_tensor_tensor(mA[:], mA[:], 1.0, per_tok(gT), ALU.add, ALU.mult))
        dve.wait_ge(S("xT_act"), 4)
        dve.wait_ge(S("xT_dve"), 4)
        step(v.tensor_tensor(H[:, :, SEQ:TOK], H[:, :, SEQ:TOK], mA[:, :, 1:9], ALU.mult))
        step(v.tensor_tensor(H[:, :, SEQ:TOK], H[:, :, SEQ:TOK], mB[:, :, 1:9], ALU.add))

        def act_low(k):
            dve.wait_ge(S("act_hi_ready"), k + 1)
            v.tensor_tensor(act_lo[:, k, :], H[:, k, :], act_hi[:, k, :].bitcast(F32), ALU.subtract
                            ).then_inc(S("act_lo_ready"), 1)

        for k in range(KT):
            v.tensor_scalar(H[:, k, 0:SEQ], H[:, k, 0:SEQ], mA[:, k, 0:1], mB[:, k, 0:1], ALU.mult, ALU.add
                            ).then_inc(S("H_ready"), 1)
            if k:
                act_low(k - 1)
        act_low(KT - 1)

        def rope(q, p, fills, dst, ready, ready_n):
            dve.wait_ge(unit_done[p], q + 1)
            v.tensor_tensor(halves(dst), accv[p], halves(cosT[:]), ALU.mult)
            v.tensor_tensor(halves(swp[0:64, :]), accv[p][64:128], halves(sinT[64:128, :]), ALU.mult)
            v.tensor_tensor(halves(swp[64:128, :]), accv[p][0:64], halves(sinT[0:64, :]), ALU.mult
                            ).then_inc(acc_free[p], 1)
            dve.wait_ge(acc_free[p], fills + 1)
            v.tensor_tensor(dst, dst, swp[:], ALU.add).then_inc(ready, 1)
            dve.wait_ge(ready, ready_n)

        dve.wait_ge(unit_done[0], Q_A + 1)
        v.tensor_scalar(halves(wiT[:]), accv[0][0:HEADS], IDX_SCALE, None, ALU.mult).then_inc(acc_free[0], 1)
        dve.wait_ge(S("rope_landed"), 32)
        rope(Q_A, 1, N_A, kiT[:], S("ki_ready"), 1)
        step(v.memset(accS[:, P:1280], 0.0))
        for b in (1, 2, 3):
            last = v.tensor_scalar(accS[:, OFF[b] + b * P:OFF[b] + (b + 1) * P], tri[:], 1e8, None, ALU.mult)
        step(last)

        def add_scores(h, first=False):
            dve.wait_ge(S("idx_relu"), h + 1)
            if not first:
                dve.wait_ge(S("idx_acc"), h)
            for b in (1, 2, 3):
                a = accS[:, OFF[b]:OFF[b] + (b + 1) * P]
                last = v.scalar_tensor_tensor(a, reluP[:, OFF[b]:OFF[b] + (b + 1) * P],
                                              wiq[:, bass.ds((b - 1) * HEADS + h, 1)], a, ALU.mult, ALU.add)
            last.then_inc(S("idx_acc"), 1)

        def index_query(i, p, first=False):
            h = 2 * i + p
            if not first:
                dve.wait_ge(S("idx_mm"), h - 1)
            rope(Q_A + 1 + i, p, N_A + 1 + i, qiT[p][:], S("qi_ready"), h + 1)
            v.tensor_copy(qiS[:, :, bass.ds(h, 1)], qiT[p][:, SEQ:TOK].unsqueeze(2)).then_inc(S("qiS_done"), 1)

        index_query(0, 0, first=True)
        dve.wait_ge(S("ki_T"), 1)
        v.tensor_copy(wiq, ps[:, 3, 0:48])
        v.tensor_copy(kistok[:], ps[0:NB, 1, 0:P])
        v.tensor_copy(kitok[:].rearrange("p t d -> p (t d)"), ps[:, 0, :]).then_inc(S("ki_tok_ready"), 1)
        dve.wait_ge(S("ki_tok_ready"), 1)
        index_query(0, 1, first=True)
        add_scores(0, first=True)
        with dve.Fori(1, 8) as i:
            index_query(i, 0)
            add_scores(2 * i - 1)
            index_query(i, 1)
            add_scores(2 * i)
        dve.wait_ge(S("gate_bias_landed"), 16)

        def gate_row(c):
            dve.wait_ge(S("gate_mm"), c + 1)
            v.tensor_tensor(gate_rows[:, 512 * c:512 * (c + 1)], acc[c % 2][0:9, 1, :],
                            gate_bias[:, 512 * c:512 * (c + 1)], ALU.add).then_inc(S("gate_rows_ready"), 1)

        for q in range(Q_GATE, Q_B):
            lo(q, 1)
            if q == Q_GATE + 2:
                add_scores(15)
                dve.wait_ge(S("idx_acc"), 16)
            c = (q - Q_GATE) // 2
            if q % 2 == Q_GATE % 2 and c >= 2:
                gate_row(c - 2)
        gate_row(2)
        rounds = [(b, r) for b in (1, 2, 3) for r in range(TOPK_P // 8)]

        def prompt_round(b):
            a = accS[:, OFF[b]:OFF[b] + (b + 1) * P]
            step(v.max(max8, a))
            step(v.match_replace(a, max8, a, TAKEN))

        def kv_rows(j):
            dve.wait_ge(S("kv_T"), j + 1)
            dst, s = (ktok, 0) if j < 4 else (vtok, 1)
            c = (j % 4) * P
            v.tensor_copy(dst[:, :, c:c + P], ps[:, j % 2, :].rearrange("p (t d) -> p t d", d=P))
            v.tensor_copy(stok[:, s, c:c + P], ps[0:NB, 2 + j % 2, 0:P]).then_inc(S("kv_evac"), 1)

        for j in range(8):
            q, p = Q_B + j // 2, j % 2
            if j < 4:
                rope(q, p, N_B + j // 2, kT[:, j, :], S("kv_ready"), j + 1)
            else:
                if j == 4:
                    dve.wait_ge(S("gate_stored"), 16)
                dve.wait_ge(unit_done[p], q + 1)
                dve.wait_ge(S("kv_T"), j - 1)
                v.tensor_copy(halves(vT[p][:]), accv[p]).then_inc(S("kv_ready"), 1)
            if j == 0:
                gate_row(3)
            if j:
                kv_rows(j - 1)
            for b, _ in rounds[6 * j:6 * j + 6]:
                prompt_round(b)
        kv_rows(7)
        v.tensor_copy(maskb[:, 0:P], tri[:])
        for b in (1, 2, 3):
            last = v.tensor_scalar(maskb[:, OFF[b]:OFF[b] + (b + 1) * P], accS[:, OFF[b]:OFF[b] + (b + 1) * P],
                                   -2e38, MASKED, ALU.is_gt, ALU.mult)
        last.then_inc(S("mask_ready"), 1)
        dve.wait_ge(S("out_front"), 6 * 16)
        step(v.memset(wiD[:], 0.0))
        v.tensor_copy(wiD[:].rearrange("h a b -> h (a b)")[:, 0:64:9], wiT[:, SEQ:TOK]).then_inc(S("wiD_ready"), 1)
        for b in range(NB):
            dve.wait_ge(S("si_T"), b + 1)
            v.tensor_copy(kiTb[:, 1024:2048], ps[:, 2:4, :].rearrange("p a n -> p (a n)"))
            v.tensor_copy(kiTb[:, PAST:PAST + 1], kiT[:, SEQ + b:SEQ + b + 1]).then_inc(S("si_kd"), 1)
            dve.wait_ge(S("si_hr"), b + 1)
            src, one = ps[0:NB, :, :].rearrange("p a n -> p (a n)"), acc[1][0:NB, 0, 0:1]
            if b == 0:
                v.tensor_copy(scoreS[:, 0:PAST], src)
                v.tensor_copy(scoreS[:, PAST:PAST + 1], one).then_inc(S("si_sum"), 1)
            else:
                v.tensor_tensor(scoreS[:, 0:PAST], src, scoreS[:, 0:PAST], ALU.add)
                v.tensor_tensor(scoreS[:, PAST:PAST + 1], one, scoreS[:, PAST:PAST + 1], ALU.add
                                ).then_inc(S("si_sum"), 1)
            dve.wait_ge(S("si_sum"), b + 1)
        step(v.memset(qSm[:], 0.0))

        def evac(h, hp1):
            dve.wait_ge(S("attn_pv"), hp1)
            dve.wait_ge(S("sga_ready"), hp1)
            v.tensor_tensor(silu_ga[:, h, 0:SEQ], ps[:, 3, :], silu_ga[:, h, 0:SEQ], ALU.mult
                            ).then_inc(S("attn_evac"), 1)

        def pt_copy(hp1):
            dve.wait_ge(S("attn_T"), hp1)
            v.tensor_copy(probT[:, 512:1024], ps[:, 1, :])
            v.tensor_copy(probT[:, 1024:1280], ps[:, 2, 0:256]).then_inc(S("pt_dve"), 1)

        def body_c(h, first=False):
            q = Q_C + h
            rope(q, 0, N_C + h, qT[:], S("q_ready"), h + 1)
            kv = h // 4
            v.tensor_copy(qSm[:].rearrange("p b k h -> p b (k h)")[:, :, bass.ds(kv * HEADS + h, 1)],
                          qT[:, SEQ:TOK].unsqueeze(2))
            if not first:
                pt_copy(h)
            dve.wait_ge(S("ega_ready"), h + 1)
            step(v.tensor_scalar(ebuf[:], ebuf[:], 1.0, None, ALU.add))
            step(v.reciprocal(ebuf[:], ebuf[:]))
            v.tensor_tensor(halves(silu_ga[:, h, :]), accv[1], halves(ebuf[:]), ALU.mult).then_inc(acc_free[1], 1)
            dve.wait_ge(acc_free[1], N_C + h + 1)
            v.tensor_copy(sgaS[:, h, :], silu_ga[:, h, SEQ:TOK]).then_inc(S("sga_ready"), 1)
            if not first:
                evac(h - 1, h)
            dve.wait_ge(S("attn_qk"), h + 1)
            for b in range(4):
                bank, c = S_AT[b]
                last = v.reduce_max(mxq[:, b:b + 1], ps[:, bank, c:c + (b + 1) * P], AX.X)
            step(last)
            v.tensor_scalar(nmq, mxq, -ATT_SCALE, None, ALU.mult).then_inc(S("nm_ready"), 1)
            dve.wait_ge(S("exp_done"), h + 1)
            step(v.reciprocal(rq, sumq))
            for b in range(4):
                a = prob[:, OFF[b]:OFF[b] + (b + 1) * P]
                last = v.tensor_scalar(a, a, rq[:, b:b + 1], None, ALU.mult)
            last.then_inc(S("prob_ready"), 1)

        chain.enter(0, 0, 4)
        body_c(0, first=True)
        chain.leave(1)
        with dve.Fori(1, HEADS) as h:
            chain.enter(h, 1, 4)
            body_c(h)
        chain.leave(HEADS - 1)
        pt_copy(HEADS)
        evac(HEADS - 1, HEADS)
        dve.wait_ge(S("attn_evac"), HEADS)
        dve.wait_ge(S("att_stored"), HEADS * 16)
        v.memset(ub[0][:, 0:16], 0.0)
        v.memset(ub[1][:, 0:16], 0.0).then_inc(S("front_done"), 1)

        def sample_round(dst):
            a = scoreS[:, 0:PAST + 1]
            step(v.max(max8[0:NB], a))
            step(v.max_index(idx8[:], max8[0:NB], a))
            v.tensor_copy(dst, idx8[:])
            step(v.match_replace(a, max8[0:NB], a, TAKEN))

        dve.wait_ge(S("front_done"), 1)
        for g, w in enumerate(WINDOWS):
            for p in range(2):
                j = 2 * g + p
                dve.wait_ge(unit_done[p], Q_D + 2 * g + 1)
                if j >= 2:
                    dve.wait_ge(S("u_T"), j - 1)
                v.tensor_copy(ub[p][:, 16:16 + HALF], acc[p][:, 0, 0:HALF])
                v.tensor_copy(ub[p][:, 16 + HALF:16 + SEQ], acc[p][:, 1, 0:SEQ - HALF])
                v.tensor_copy(ext[p][:, :, 15:16], acc[p][:, 1, SEQ - HALF:HALF].unsqueeze(2)).then_inc(acc_free[p], 1)
                dve.wait_ge(S("state_T"), j + 1)
                v.tensor_copy(ext[p][:, :, 0:STATE],
                              ps[:, p, 0:NB * STATE].rearrange("p (b s) -> p b s", s=STATE)).then_inc(S("u_ready"), 1)
                dve.wait_ge(S("u_ready"), j + 1)
                src, s = ub[p], 1
                n = 0
                while s < w:
                    step(v.tensor_tensor(win[n % 2][:, 2 * s - 1:], src[:, 2 * s - 1:], src[:, s - 1:16 + SEQ - s],
                                         ALU.add))
                    src, s, n = win[n % 2], 2 * s, n + 1
                if j >= 2:
                    dve.wait_ge(S("mix_mm"), 2 * g)
                r = win[n % 2]
                step(v.tensor_tensor(r[:, 0:16], src[:, 16:32], rcnt[:, 16 * g:16 * g + 16], ALU.mult))
                v.tensor_tensor(pooled[:, p, 0:16], r[:, 0:16], ub[p][:, 16:32], ALU.subtract)
                v.scalar_tensor_tensor(pooled[:, p, 16:SEQ], src[:, 32:16 + SEQ], 1.0 / w, ub[p][:, 32:16 + SEQ],
                                       ALU.mult, ALU.subtract)
                step(v.tensor_reduce(wsum8[:], ext[p][:, :, 16 - w:16], AX.X, ALU.add))
                v.scalar_tensor_tensor(pooled[:, p, SEQ:TOK], wsum8[:], 1.0 / w, ext[p][:, :, 15], ALU.mult,
                                       ALU.subtract).then_inc(S("pooled_ready"), 1)
                if j >= 2 and p == 0:
                    dve.wait_ge(S("out_pool"), 16 * (2 * g + 1))
                dve.wait_ge(S("u_T"), j + 1)
                v.tensor_copy(pstage[:, p * P:(p + 1) * P], ps[0:STATE, p, 128:256])
                v.tensor_copy(sstage[:, p * P:(p + 1) * P], ps[0:NB, p, 256:384]).then_inc(S("u_tok_ready"), 1)
                sample_round(idxS[:, 8 * (4 * g + p):8 * (4 * g + p) + 8])
            for p in range(2):
                j = 2 * g + p
                dve.wait_ge(S("egb_ready"), j + 1)
                step(v.tensor_scalar(e_back[:], e_back[:], 1.0, None, ALU.add))
                step(v.reciprocal(e_back[:], e_back[:]))
                if j:
                    dve.wait_ge(S("pool_hi_ready"), j)
                v.tensor_tensor(halves(e_back[:]), accv[p], halves(e_back[:]), ALU.mult).then_inc(acc_free[p], 1)
                dve.wait_ge(acc_free[p], N_D + 2 * g + 2)
                dve.wait_ge(S("mix_mm"), j + 1)
                v.scalar_tensor_tensor(halves(s_back[:]), ps[:, 2:4, 0:HALF], spT[:, j:j + 1], halves(e_back[:]),
                                       ALU.mult, ALU.mult).then_inc(S("pg_ready"), 1)
                dve.wait_ge(S("pool_hi_ready"), j + 1)
                dve.wait_ge(S("pg_ready"), j + 1)
                v.tensor_tensor(pool_lo[:, j, :], s_back[:], pool_hi[:, j, :].bitcast(F32), ALU.subtract
                                ).then_inc(S("pool_ready"), 1)
                sample_round(idxS[:, 8 * (4 * g + 2 + p):8 * (4 * g + 2 + p) + 8])
        with dve.Fori(0, KT) as j:
            a = scoreS[:, 0:PAST + 1]
            chain.enter(j, 0, 5)
            step(v.max(max8[0:NB], a))
            dve.wait_ge(acc_free[0], N_E + j + 1)
            chain.count(v.tensor_scalar(e_back[:], e_back[:], 1.0, None, ALU.add))
            step(v.max_index(idx8[:], max8[0:NB], a))
            v.reciprocal(s_back[:], e_back[:]).then_inc(S("smb_ready"), 1)
            chain.count(v.tensor_copy(idxS[:, bass.ds(8 * j + 128, 8)], idx8[:]))
            step(v.match_replace(a, max8[0:NB], a, TAKEN))
            dve.wait_ge(S("smb_ready"), j + 1)
            dve.wait_ge(unit_done[1], Q_E + j + 1)
            v.tensor_tensor(halves(big2[:, j, :]), accv[1], halves(s_back[:]), ALU.mult).then_inc(acc_free[1], 1)
        chain.leave(KT)
        dve.wait_ge(unit_done[1], Q_F1)
        dve.wait_ge(S("pt_landed"), 16)
        r = [rowf[:, n, :] for n in range(6)]
        step(v.tensor_copy(ptf[:], pti[:]))
        step(v.tensor_copy(r[0], idxS[:]))
        v.tensor_scalar(r[3], r[0], float(PAST), 1e6, ALU.is_ge, ALU.mult)
        step(v.tensor_scalar(r[1].bitcast(U32), idxS[:], 7, None, ALU.logical_shift_right))
        step(v.tensor_copy(r[2], r[1].bitcast(U32)))
        step(v.scalar_tensor_tensor(r[3], r[2], -float(P), r[3], ALU.mult, ALU.add))
        step(v.tensor_tensor(r[3], r[3], r[0], ALU.add))
        for pg in range(PAGES):
            step(v.tensor_scalar(r[4], r[2], float(pg), ptf[:, pg:pg + 1], ALU.is_equal, ALU.mult))
            step(v.scalar_tensor_tensor(r[3], r[4], float(P), r[3], ALU.mult, ALU.add))
        v.tensor_copy(r[5], r[3]).then_inc(S("rowf_ready"), 1)
        dve.wait_ge(S("rowf_T"), 1)
        v.tensor_copy(rowT[:].rearrange("p a b -> p (a b)"), ps[:, 3, 0:2 * NB]).then_inc(S("rows_ready"), 1)
        for b in range(NB):
            dve.wait_ge(S("sa_T"), b + 1)
            v.tensor_copy(kselT[:, 2:4, :].rearrange("p a n -> p (a n)"), ps[:, 1, :]).then_inc(S("sa_kd"), 1)
            dve.wait_ge(S("sa_qk"), b + 1)
            step(v.reduce_max(mxq[0:HEADS, 0:1], ps[0:HEADS, 2, 0:256], AX.X))
            v.tensor_scalar(nmq[0:HEADS, 0:1], mxq[0:HEADS, 0:1], -ATT_SCALE, None, ALU.mult).then_inc(S("sa_nm"), 1)
            dve.wait_ge(S("sa_exp"), b + 1)
            step(v.reciprocal(rq[0:HEADS, 0:1], sumq[0:HEADS, 0:1]))
            v.tensor_scalar(pS[:], pS[:], rq[0:HEADS, 0:1], None, ALU.mult).then_inc(S("sa_prob"), 1)
            dve.wait_ge(S("sa_pT"), b + 1)
            v.tensor_copy(pST[:].rearrange("p a h -> p (a h)"), ps[:, 2, 256:256 + 2 * HEADS]).then_inc(S("sa_pst"), 1)
            dve.wait_ge(S("sa_pv"), b + 1)
            v.tensor_tensor(attS[:, :, b], ps[:, 3, 64:64 + HEADS], sgaS[:, :, b], ALU.mult).then_inc(S("attS_ready"), 1)
        with dve.Fori(0, 8) as i:
            chain.enter(i, 0, 2)
            for p in range(2):
                dve.wait_ge(acc_free[p], N_F1 + i + 1)
                step(v.tensor_scalar(e_back[:], e_back[:], 1.0, None, ALU.add))
                v.reciprocal(big1[:, 2 * i + p, :], e_back[:]).then_inc(S("sma_ready"), 1)
        chain.leave(8)
        for k in range(KT):
            dve.wait_ge(S("att_hi_ready"), k + 1)
            v.tensor_tensor(act_lo[:, k, 0:SEQ], att_stage[k % 4][:], act_hi[:, k, 0:SEQ].bitcast(F32), ALU.subtract)
            v.tensor_tensor(act_lo[:, k, SEQ:TOK], attS[:, k, :], act_hi[:, k, SEQ:TOK].bitcast(F32), ALU.subtract
                            ).then_inc(S("att_split"), 1)
        with dve.Fori(0, 8) as i:
            for p in range(2):
                j = 2 * i + p
                dve.wait_ge(unit_done[p], Q_F2 + i + 1)
                v.tensor_tensor(halves(big1[:, j, :]), accv[p], halves(big1[:, j, :]), ALU.mult).then_inc(acc_free[p], 1)
                dve.wait_ge(acc_free[p], N_F2 + i + 1)
                v.tensor_tensor(big2[:, j, :], big1[:, j, :], big2[:, j, :], ALU.add).then_inc(S("m_ready"), 1)
        v.memset(sm[:].bitcast(F32), 0.0).then_inc(S("sm_zero"), 1)
        for k in range(KT):
            dve.wait_ge(S("m_hi_ready"), k + 1)
            v.tensor_tensor(act_lo[:, k, :], big2[:, k, :], act_hi[:, k, :].bitcast(F32), ALU.subtract
                            ).then_inc(S("m_split"), 1)
        dve.wait_ge(S("sm_hi_ready"), 1)
        v.tensor_tensor(sm[:, :, NB:2 * NB], big2[:, :, SEQ:TOK], sm[:, :, 0:NB].bitcast(F32), ALU.subtract
                        ).then_inc(S("sm_ready"), 1)
        lo(Q_G, 1)
        lo(Q_G + 1, 1)
        dve.wait_ge(S("g_landed"), 48)
        dve.wait_ge(S("xs2_landed"), 16)

        def chunk(c, last=False):
            dve.wait_ge(S("xch_landed"), 16 * (c + 1))
            for i in range(4):
                y = yrow[:, i, bass.ds(512 * c, 512)]
                dve.wait_ge(S("y_mm"), 5 * c + i + 1)
                v.tensor_tensor(y, ps[:, i, :], gate_p[:, bass.ds(512 * c, 512)], ALU.mult).then_inc(S("y_free"), 1)
                dve.wait_ge(S("y_free"), 5 * c + i + 1)
                v.tensor_tensor(y, y, xch[:, i, :], ALU.add).then_inc(S("y_added"), 1)
            dve.wait_ge(S("y_mm"), 5 * c + 5)
            v.tensor_copy(srow[:], acc[0][0:16, 0, :]).then_inc(S("srow_ready"), 1)
            dve.wait_ge(unit_done[1], Q_G + 2 * c + 2)
            v.tensor_tensor(srow[0:NB, :], acc[0][0:NB, 1, :], gate_s[:, bass.ds(512 * c, 512)], ALU.mult
                            ).then_inc(S("y_free"), 1)
            dve.wait_ge(S("y_free"), 5 * c + 5)
            y = ys[:, bass.ds(512 * c, 512)]
            v.tensor_tensor(y, y, srow[0:NB, :], ALU.add).then_inc(S("ys_added"), 1)

        with dve.Fori(0, 3) as c:
            chunk(c)
            lo(Q_G + 2 * c + 2, 1)
            lo(Q_G + 2 * c + 3, 1)
        chunk(3)
        dve.wait_ge(S("ys_added"), 4)
        dve.wait_ge(S("y_added"), 16)
        v.memset(max8, 0.0).then_inc(S("y_all"), 1)
        for i in range(5):
            n = P if i < 4 else NB
            y = yrow[:, i, :] if i < 4 else ys[:]
            inverse_root(n, i, i + 6)
            v.scalar_tensor_tensor(y, y, rstd[0:n, i:i + 1], gfin[0:n, :], ALU.mult, ALU.mult).then_inc(S("y_ready"), 1)

    @block.tensor
    def _(pe):
        mm = nc.tensor.matmul

        def tile(q, p, fills, kt=KT, hi_=act_hi, lo_=act_lo, parts=None, free=True):
            if free:
                pe.wait_ge(acc_free[p], fills)
            pe.wait_ge(lo_ready[p], q + 1)
            for k in range(kt):
                if parts is not None:
                    pe.wait_ge(parts, k + 1)
                wh, wl = whi[p][:, k * P:(k + 1) * P], wlo[p][:, k * P:(k + 1) * P]
                for n, (w, x) in enumerate(((wh, hi_), (wh, lo_), (wl, hi_))):
                    for a in range(2):
                        last = mm(acc[p][:, a, 0:HALF], w, x[:, k, a * HALF:(a + 1) * HALF],
                                  start=(k == 0 and n == 0), stop=(k == kt - 1 and n == 2))
            last.then_inc(unit_done[p], 1)

        def cond_chunk(q0, bank):
            for kq in range(4):
                q, p = q0 + kq // 2, kq % 2
                pe.wait_ge(lo_ready[p], q + 1)
                for kk in range(4):
                    for w in (whi, wlo):
                        last = mm(bank, cst[:, 4 * kq + kk, :], w[p][:, kk * 512:(kk + 1) * 512],
                                  start=(kq == 0 and kk == 0 and w is whi), stop=(kq == 3 and kk == 3 and w is wlo))
                last.then_inc(unit_done[p], 1)

        tr = nc.tensor.transpose
        pe.wait_ge(S("tables_landed"), 9 * 16)
        tr(ps[:, 0, 0:128], rows_cs[:], ident[:])
        tr(ps[:, 1, 0:16], rows_cp[:], ident[0:16, 0:16])
        tr(ps[:, 1, 16:64], rows_b[:], ident[0:48, 0:48])
        tr(ps[:, 1, 64:88], rows_gs[:], ident[0:24, 0:24]).then_inc(S("rows_T"), 1)
        pe.wait_ge(S("cst_ready"), 1)

        def mod_columns(n):
            pe.wait_ge(acc_free[n % 2], n // 2 + 1)
            for m in range(4):
                last = mm(modT[:, 4 * n + m, :], modb[n % 2][:, m * P:(m + 1) * P], sel9, start=True, stop=True)
            last.then_inc(S("mod_mm"), 1)

        for n in range(8):
            if n >= 2:
                pe.wait_ge(acc_free[n % 2], n // 2)
            cond_chunk(2 * n, acc[n % 2][:, 0, :])
            if n == 0:
                pe.wait_ge(S("xs_ready"), 1)
                for k in range(KT):
                    last = tr(xsT[:, k, :], xs[:, k * P:(k + 1) * P], ident[0:NB, 0:NB])
                last.then_inc(S("xs_T"), 1)
            if n:
                mod_columns(n - 1)
            if n in (1, 2, 3, 4):
                i = n - 1
                pe.wait_ge(S("xhat_ready"), i + 1)
                if i:
                    pe.wait_ge(S("xT_act"), i)
                    pe.wait_ge(S("xT_dve"), i)
                for k in range(KT):
                    last = tr(ps[:, k // 4, (k % 4) * P:(k % 4 + 1) * P], x_tok[:, i, k * P:(k + 1) * P], ident[:])
                last.then_inc(S("xT_done"), 1)
        mod_columns(7)
        tile(Q_A, 0, N_A, parts=S("act_lo_ready"))
        tile(Q_A, 1, N_A)

        def score(h, p):
            pe.wait_ge(S("qi_ready"), h + 1)
            pe.wait_ge(S("idx_relu"), h)
            for b in (1, 2, 3):
                last = mm(ps[:, b - 1, 0:(b + 1) * P], qiT[p][:, b * P:(b + 1) * P], kiT[:, 0:(b + 1) * P],
                          start=True, stop=True)
            last.then_inc(S("idx_mm"), 1)

        tile(Q_A + 1, 0, N_A + 1)
        pe.wait_ge(S("ki_ready"), 1)
        for b in (1, 2, 3):
            tr(ps[:, 3, (b - 1) * 16:b * 16], wiT[:, b * P:(b + 1) * P], ident[0:HEADS, 0:HEADS])
        tr(ps[0:NB, 1, 0:P], kiT[:, SEQ:TOK], ident[:])
        for b in range(4):
            last = tr(ps[:, 0, b * P:(b + 1) * P], kiT[:, b * P:(b + 1) * P], ident[:])
        last.then_inc(S("ki_T"), 1)
        tile(Q_A + 1, 1, N_A + 1)
        pe.wait_ge(S("ki_tok_ready"), 1)
        score(0, 0)
        with pe.Fori(1, 8) as i:
            tile(Q_A + 1 + i, 0, N_A + 1 + i)
            score(2 * i - 1, 1)
            tile(Q_A + 1 + i, 1, N_A + 1 + i)
            score(2 * i, 0)

        def gate_mm(c):
            pe.wait_ge(S("gate_part"), c + 1)
            mm(acc[c % 2][0:9, 1, :], sel9, modb[c % 2][:], start=True, stop=True).then_inc(S("gate_mm"), 1)

        for c in range(4):
            if c < 2:
                pe.wait_ge(acc_free[c % 2], N_GATE)
            else:
                pe.wait_ge(S("gate_rows_ready"), c - 1)
            cond_chunk(Q_GATE + 2 * c, acc[c % 2][:, 0, :])
            if c == 0:
                score(15, 1)
            if c:
                gate_mm(c - 1)
        def kv_transpose(j):
            pe.wait_ge(S("kv_ready"), j + 1)
            if j >= 2:
                pe.wait_ge(S("kv_evac"), j - 1)
            else:
                pe.wait_ge(S("idx_relu"), HEADS)
            src = kT[:, j, :] if j < 4 else vT[j % 2][:]
            for b in range(4):
                tr(ps[:, j % 2, b * P:(b + 1) * P], src[:, b * P:(b + 1) * P], ident[:])
            tr(ps[0:NB, 2 + j % 2, 0:P], src[:, SEQ:TOK], ident[:]).then_inc(S("kv_T"), 1)

        for j in range(8):
            if j == 0:
                pe.wait_ge(S("gate_rows_ready"), 3)
            if j == 1:
                pe.wait_ge(S("gate_rows_ready"), 4)
            if j >= 6:
                pe.wait_ge(S("kv_ready"), j - 1)
            tile(Q_B + j // 2, j % 2, N_B + j // 2, free=2 <= j < 6)
            if j == 0:
                gate_mm(3)
            if j:
                kv_transpose(j - 1)
        kv_transpose(7)
        pe.wait_ge(S("kv_evac"), 8)
        pe.wait_ge(acc_free[0], N_C)
        pe.wait_ge(acc_free[1], N_C)
        pe.wait_ge(S("wiD_ready"), 1)
        for b in range(NB):
            pe.wait_ge(S("kib_landed"), 16 * PAGES * (b + 1))
            if b:
                pe.wait_ge(S("si_sum"), b)
            for pg in range(PAGES):
                last = tr(ps[:, pg // 4, (pg % 4) * P:(pg % 4 + 1) * P], kib[:, pg, :], ident[:])
            last.then_inc(S("si_T"), 1)
            pe.wait_ge(S("si_ka"), b + 1)
            pe.wait_ge(S("si_kd"), b + 1)
            for n in range(4):
                mm(ps[0:HEADS, n, :], qiS[:, b, :], kiTb[:, 512 * n:512 * (n + 1)], start=True, stop=True)
            mm(acc[0][0:HEADS, 0, 0:1], qiS[:, b, :], kiTb[:, PAST:PAST + 1], start=True, stop=True
               ).then_inc(S("si_qk"), 1)
            pe.wait_ge(S("si_relu"), b + 1)
            for n in range(4):
                mm(ps[0:NB, n, :], wiD[:, b, :], reluS[:, 512 * n:512 * (n + 1)], start=True, stop=True)
            mm(acc[1][0:NB, 0, 0:1], wiD[:, b, :], reluS[:, PAST:PAST + 1], start=True, stop=True
               ).then_inc(S("si_hr"), 1)
        pe.wait_ge(S("si_sum"), NB)
        pe.wait_ge(S("mask_ready"), 1)
        pe.wait_ge(S("identb_ready"), 1)

        def transpose_prob(hp1):
            pe.wait_ge(S("prob_ready"), hp1)
            for (qb, kb), n in PT_AT.items():
                last = tr(ps[:, n // 4, (n % 4) * P:(n % 4 + 1) * P],
                          prob[:, OFF[qb] + kb * P:OFF[qb] + (kb + 1) * P], ident[:])
            last.then_inc(S("attn_T"), 1)

        def values(hp1):
            pe.wait_ge(S("pt_act"), hp1)
            pe.wait_ge(S("pt_dve"), hp1)
            pe.wait_ge(S("vcur_ready"), hp1)
            pe.wait_ge(S("attn_evac"), hp1 - 1)
            for kb in range(4):
                n = PT_AT[kb, kb]
                last = mm(ps[:, 3, kb * P:512], vcur[:, kb, :], probT[:, n * P:(n + 4 - kb) * P],
                          start=(kb == 0), stop=(kb == 3))
            last.then_inc(S("attn_pv"), 1)

        def logits(h):
            pe.wait_ge(S("q_ready"), h + 1)
            for b in range(4):
                bank, c = S_AT[b]
                o = ps[:, bank, c:c + (b + 1) * P]
                mm(o, identb[:], maskb[:, OFF[b]:OFF[b] + (b + 1) * P], start=True, stop=False)
                last = mm(o, qT[:, b * P:(b + 1) * P],
                          kT[:].rearrange("p k n -> p (k n)")[:, bass.ds((h // 4) * TOK, (b + 1) * P)]
                          if not isinstance(h, int) else kT[:, h // 4, 0:(b + 1) * P], start=False, stop=True)
            last.then_inc(S("attn_qk"), 1)

        tile(Q_C, 0, N_C)
        tile(Q_C, 1, N_C)
        logits(0)
        with pe.Fori(1, HEADS) as h:
            tile(Q_C + h, 0, N_C + h)
            transpose_prob(h)
            tile(Q_C + h, 1, N_C + h)
            values(h)
            logits(h)
        transpose_prob(HEADS)
        values(HEADS)
        for g in range(4):
            q = Q_D + 2 * g
            for p in range(2):
                j = 2 * g + p
                tile(q, p, N_D + 2 * g)
                if j == 0:
                    pe.wait_ge(S("pool_landed"), 32)
                    pe.wait_ge(S("attn_evac"), HEADS)
                if j >= 2:
                    pe.wait_ge(S("u_tok_ready"), j - 1)
                tr(ps[:, p, 0:NB * STATE], state[:, j * P:(j + 1) * P], ident[0:120, 0:120]).then_inc(S("state_T"), 1)
                pe.wait_ge(S("u_ready"), j + 1)
                tr(ps[0:STATE, p, 128:256], ub[p][:, 16 + SEQ - STATE:16 + SEQ], ident[:])
                tr(ps[0:NB, p, 256:384], ext[p][:, :, 15], ident[:]).then_inc(S("u_T"), 1)
            for p in range(2):
                j = 2 * g + p
                tile(q + 1, p, N_D + 2 * g + 1)
                pe.wait_ge(S("pooled_ready"), 2 * g + 2)
                if j:
                    pe.wait_ge(S("pg_ready"), j)
                for a in range(2):
                    for c in range(2):
                        last = mm(ps[:, 2 + a, 0:HALF], wpool[:, g, c, p * P:(p + 1) * P],
                                  pooled[:, c, a * HALF:(a + 1) * HALF], start=(c == 0), stop=(c == 1))
                last.then_inc(S("mix_mm"), 1)
        pe.wait_ge(S("pool_ready"), 8)
        with pe.Fori(0, KT) as j:
            tile(Q_E + j, 0, N_E + j)
            tile(Q_E + j, 1, N_E + j, kt=8, hi_=pool_hi, lo_=pool_lo)
        pe.wait_ge(S("rowf_ready"), 1)
        for hf in range(2):
            last = tr(ps[:, 3, hf * NB:(hf + 1) * NB], rowf[:, 5, hf * P:(hf + 1) * P], ident[0:NB, 0:NB])
        last.then_inc(S("rowf_T"), 1)
        for b in range(NB):
            pe.wait_ge(S("sa_sel"), 64 * (b + 1))
            for kv in range(KVH):
                for hf in range(2):
                    last = tr(ps[:, kv // 2, (kv % 2) * 256 + hf * P:(kv % 2) * 256 + (hf + 1) * P],
                              ksel[:, hf, kv * P:(kv + 1) * P], ident[:])
            last.then_inc(S("sa_T"), 1)
            pe.wait_ge(S("sa_ka"), b + 1)
            pe.wait_ge(S("sa_kd"), b + 1)
            for kv in range(KVH):
                last = mm(ps[0:HEADS, 2, 0:256], qSm[:, b, kv, :], kselT[:, kv, :], start=(kv == 0), stop=(kv == 3))
            last.then_inc(S("sa_qk"), 1)
            pe.wait_ge(S("sa_prob"), b + 1)
            for hf in range(2):
                last = tr(ps[:, 2, 256 + hf * HEADS:256 + (hf + 1) * HEADS], pS[:, hf * P:(hf + 1) * P],
                          ident[0:HEADS, 0:HEADS])
            last.then_inc(S("sa_pT"), 1)
            pe.wait_ge(S("sa_pst"), b + 1)
            if b:
                pe.wait_ge(S("attS_ready"), b)
            else:
                pe.wait_ge(S("rows_ready"), 1)
            for kv in range(KVH):
                for hf in range(2):
                    last = mm(ps[:, 3, 64 + 4 * kv:68 + 4 * kv], vsel[:, hf, kv * P:(kv + 1) * P],
                              pST[:, hf, 4 * kv:4 * kv + 4], start=(hf == 0), stop=(hf == 1))
            last.then_inc(S("sa_pv"), 1)
        with pe.Fori(0, 8) as i:
            tile(Q_F1 + i, 0, N_F1 + i)
            tile(Q_F1 + i, 1, N_F1 + i)
        tile(Q_F2, 0, N_F2, parts=S("att_split"))
        tile(Q_F2, 1, N_F2)
        with pe.Fori(1, 8) as i:
            tile(Q_F2 + i, 0, N_F2 + i)
            tile(Q_F2 + i, 1, N_F2 + i)

        def out_chunk(c, first=False):
            for kq in range(4):
                q, p = Q_G + 2 * c + kq // 2, kq % 2
                pe.wait_ge(lo_ready[p], q + 1)
                for i in range(5):
                    if kq == 0:
                        if not first:
                            pe.wait_ge(S("y_free"), 5 * c - 4 + i)
                        elif i in (0, 4):
                            pe.wait_ge(acc_free[0], N_G)
                            pe.wait_ge(S("attS_ready"), NB)
                    for kk in range(4):
                        k = 4 * kq + kk
                        if first and i == 0:
                            pe.wait_ge(S("m_split"), k + 1)
                        if first and i == 4 and k == 0:
                            pe.wait_ge(S("sm_ready"), 1)
                        wh, wl = (w[p][:, kk * 512:(kk + 1) * 512] for w in (whi, wlo))
                        if i < 4:
                            s = slice(i * P, (i + 1) * P)
                            trio = ((act_hi[:, k, s], wh), (act_hi[:, k, s], wl), (act_lo[:, k, s], wh))
                            o = ps[:, i, :]
                        else:
                            trio = ((sm[:, k, :], wh), (sm[:, k, :], wl))
                            o = acc[0][:, 0, :]
                        for n, (x, w) in enumerate(trio):
                            last = mm(o, x, w, start=(k == 0 and n == 0), stop=(k == KT - 1 and n == len(trio) - 1))
                    if kq == 3 and i < 4:
                        last.then_inc(S("y_mm"), 1)
                if kq < 3:
                    last.then_inc(unit_done[p], 1)
            last.then_inc(S("y_mm"), 1)
            pe.wait_ge(S("srow_ready"), c + 1)
            mm(acc[0][0:64, 1, :], sel8, srow[:], start=True, stop=True).then_inc(unit_done[1], 1)

        out_chunk(0, first=True)
        with pe.Fori(1, 4) as c:
            out_chunk(c)

    ctx.close()


_INS = ['x_prompt', 'x_sample', 'c_prompt', 'c_sample', 'cache_k', 'cache_v', 'cache_kidx', 'state_pool', 'page_table',
        'g_norm', 'w_ada', 'b_ada', 'w_in', 'w_pool', 's_pool', 'w_a_proj', 'w_b_proj', 'w_out', 'g_final']
_OUTS = [('y_p', (SEQ, D), (1, SEQ, D)), ('y_s', (NB, D), (NB, 1, D)),
         ('k_p', (SEQ, 512), (1, 1, SEQ, KVH, P)), ('v_p', (SEQ, 512), (1, 1, SEQ, KVH, P)),
         ('kidx_p', (SEQ, P), (1, 1, SEQ, P)), ('pool_p', (STATE, PW), (1, 1, STATE, PW)),
         ('k_s', (NB, 512), (1, NB, 1, KVH, P)), ('v_s', (NB, 512), (1, NB, 1, KVH, P)),
         ('kidx_s', (NB, P), (1, NB, 1, P)), ('pool_s', (NB, STATE, PW), (1, NB, STATE, PW))]


def shape_constants():
    pos = np.concatenate([np.arange(SEQ), np.full(NB, PAST)]).astype(np.float32)
    inv = np.float32(10000.0) ** (-np.arange(64, dtype=np.float32) / np.float32(64))
    ang = pos[None, :] * inv[:, None]
    cos, sin = np.cos(ang).astype(np.float32), np.sin(ang).astype(np.float32)
    sel = np.zeros((18, 74), np.float32)
    for r in range(18):
        sel[r, r % 9] = 1.0
    for r in range(16):
        sel[r, 10 + r % 8] = 1.0
    cnt = np.stack([np.minimum(np.arange(16) + 1, w) for w in WINDOWS]).astype(np.float32)
    return {
        "k_cos": np.concatenate([cos, cos]), "k_sin": np.concatenate([sin, -sin]),
        "k_ident": np.eye(P, dtype=np.float32), "k_sel": sel,
        "k_rcnt": np.ascontiguousarray(np.broadcast_to((1.0 / cnt).astype(np.float32).reshape(1, 64), (P, 64))),
        "k_tri": np.where(np.arange(P)[None, :] > np.arange(P)[:, None], np.float32(MASKED), np.float32(0.0)),
    }


def kernel(**inputs):
    from concourse import bacc
    from concourse.bass_utils import run_bass_kernel_spmd

    nc = bacc.Bacc("TRN2", target_bir_lowering=False, num_devices=1)
    arrays = {n: np.ascontiguousarray(inputs[n]) for n in _INS}
    arrays.update(shape_constants())
    t = {n: nc.dram_tensor("in_" + n, a.shape, mybir.dt.from_np(a.dtype), kind="ExternalInput").ap()
         for n, a in arrays.items()}
    t["n_pool"] = arrays["cache_k"].shape[1]
    out = {n: nc.dram_tensor("out_" + n, shape, F32, kind="ExternalOutput").ap() for n, shape, _ in _OUTS}
    build(nc, t, out)
    r = run_bass_kernel_spmd(nc, [{"in_" + n: a for n, a in arrays.items()}], core_ids=[0])
    return tuple(r.results[0]["out_" + n].reshape(full) for n, _, full in _OUTS)
```

```python
from contextlib import ExitStack

import numpy as np
import concourse.bass as bass
import concourse.mybir as mybir

F32 = mybir.dt.float32
F32R = mybir.dt.float32r
BF16 = mybir.dt.bfloat16
U32 = mybir.dt.uint32
I32 = mybir.dt.int32
ALU = mybir.AluOpType
ACT = mybir.ActivationFunctionType
AX = mybir.AxisListType

P = 128
D = 2048
KT = D // P
SEQ = 512
NB = 8
TOK = SEQ + NB
HALF = TOK // 2
HEADS = 16
KVH = 4
PAST = 2048
PAGES = PAST // P
TOPK_P = 128
TOPK_S = 256
PW = 1024
WINDOWS = (2, 4, 8, 16)
STATE = 15
EPS = 1e-6
ATT_SCALE = P ** -0.5
IDX_SCALE = (HEADS * P) ** -0.5
MASKED = -1e30
TAKEN = -3e38
C_Q, C_K, C_V, C_QI, C_KI, C_WI = 0, 2048, 2560, 3072, 5120, 5248
C_GA, C_U, C_GB, C_MA, C_MB = 5264, 7312, 8336, 9360, 11408
CHUNKS = 4 * NB
ADA_CHUNKS = [8, 9, 10, 11, 4, 0, 5, 1, 6, 2, 7, 3]
RING = 6
ADA_UNITS = 4 * len(ADA_CHUNKS)
Q_A, Q_B, Q_C, Q_D, Q_E, Q_F1, Q_F2, Q_G, Q_END = 0, 9, 13, 29, 37, 53, 61, 69, 77
N_A, N_B, N_C, N_D, N_E, N_F1, N_F2, N_G = 0, 9, 11, 27, 35, 51, 59, 67
OFF = [0, 128, 384, 768, 1280]
S_AT = [(0, 0), (1, 0), (0, 128), (2, 0)]
PT_AT = {(qb, kb): sum(4 - k for k in range(kb)) + qb - kb for kb in range(4) for qb in range(kb, 4)}


class Chain:

    def __init__(self, eng, sem):
        self.eng, self.sem, self.base, self.k, self.per = eng, sem, 0, 0, None

    def count(self, ins):
        ins.then_inc(self.sem, 1)
        self.k += 1

    def step(self, ins):
        self.count(ins)
        self.eng.wait_ge(self.sem, self.at + self.k)

    at = 0

    def enter(self, i, first, per):
        self.base += self.k
        self.at = self.base + (i - first) * per
        self.k, self.per = 0, per

    def leave(self, times):
        assert self.k == self.per, (self.k, self.per)
        self.base += times * self.per
        self.at, self.k = self.base, 0


def build(nc, t, out):
    ctx = ExitStack()
    sem_of = {}

    def sem(name):
        if name not in sem_of:
            sem_of[name] = ctx.enter_context(nc.semaphore(name))
        return sem_of[name]

    BASE = 16512

    def at(name, off, shape, dt=F32):
        size = int(np.prod(shape[1:])) * (2 if dt == BF16 else 4)
        assert off + size <= 229368 - BASE, (name, off, size)
        return nc.alloc_sbuf_tensor_at(name, shape, dt, offset=BASE + off)

    act_hi = at("act_hi", 0, [P, KT, TOK], F32R)
    act_lo = at("act_lo", 33280, [P, KT, TOK], F32R)
    square_dump = at("square_dump", 33280, [P, D])
    raw = [at(f"raw{p}", 66560 + 8192 * p, [P, 2048]) for p in range(2)]
    whi = [at(f"whi{p}", 82944 + 8192 * p, [P, 2048], F32R) for p in range(2)]
    wlo = [at(f"wlo{p}", 99328 + 8192 * p, [P, 2048], F32R) for p in range(2)]
    A0 = 115712
    ident = at("ident", A0, [P, P])
    identb = at("identb", A0 + 512, [P, P], BF16)
    misc = at("misc", A0 + 768, [P, 512])
    qSm = at("qSm", A0 + 2816, [P, NB, KVH, HEADS])
    qiS = at("qiS", A0 + 4864, [P, NB, HEADS])
    sgaS = at("sgaS", A0 + 5376, [P, HEADS, NB])
    attS = at("attS", A0 + 5888, [P, HEADS, NB])
    A1 = A0 + 6400
    xs = at("xs", A1, [NB, D])
    scoreS = at("scoreS", A1, [NB, PAST + 8])
    ys = at("ys", A1, [NB, D])
    A2 = A1 + 8256
    TAIL = A2 + 78336
    ring = [at(f"ring{i}", 66560 + 8192 * i, [P, 2048]) for i in range(RING)]
    gate_bias = at("gate_bias", 1024, [NB + 1, D])
    gate_rows = at("gate_rows", 9216, [NB + 1, D])
    x_tok = at("x_tok", A2 + 8192, [P, 4, D])
    H = at("H", A2 + 40960, [P, KT, TOK])
    modb = [at(f"modb{c}", A2 + 74240 + 2048 * c, [NB + 1, 512]) for c in range(2)]
    mA = at("mA", TAIL, [P, KT, 9])
    mB = at("mB", TAIL + 576, [P, KT, 9])
    tri = at("tri", TAIL + 1152, [P, P])
    rows_cs = at("rows_cs", TAIL + 1664, [P, P])
    rows_cp = at("rows_cp", TAIL + 2176, [16, P])
    rows_b = at("rows_b", TAIL + 2688, [48, P])
    rows_gs = at("rows_gs", TAIL + 3200, [24, P])
    A3 = A2 + 128
    cosT = at("cosT", A3 + 8192, [P, TOK])
    sinT = at("sinT", A3 + 10272, [P, TOK])
    kiT = at("kiT", A3 + 12352, [P, TOK])
    accS = at("accS", A3 + 14432, [P, 1280])
    reluP = at("reluP", A3 + 19552, [P, 1280])
    qiT = [at(f"qiT{p}", A3 + 24672 + 2080 * p, [P, TOK]) for p in range(2)]
    swp = at("swp", A3 + 28832, [P, TOK])
    ebuf = at("ebuf", A3 + 30912, [P, TOK])
    wiT = at("wiT", A3 + 32992, [HEADS, TOK])
    kT = at("kT", A2, [P, KVH, TOK])                
    vtok = at("vtok", A3 + 35072, [P, 4, 512])   
    maskb = at("maskb", A3 + 43264, [P, 1280], BF16)
    BG = A3 + 45824
    silu_ga = at("silu_ga", BG, [P, HEADS, TOK])
    ktok = at("ktok", A3 + 52224, [P, 4, 512])
    stok = at("stok", A3 + 60416, [NB, 2, 512])
    vT = [at(f"vT{p}", A3 + 64512 + 2080 * p, [P, TOK]) for p in range(2)]
    kib = [at(f"kib{s}", BG + 2048 * s, [P, 4 * P]) for s in range(3)]
    kiTc = [at(f"kiTc{s}", A3 + 19552 + 2048 * s, [P, 512]) for s in range(2)]
    reluS = [at(f"reluS{s}", A3 + 23648 + 2048 * s, [HEADS, 512]) for s in range(2)]
    wiD = at("wiD", A3 + 27744, [HEADS, NB, NB])
    pgi = at("pgi", 0, [P, NB, PAGES], I32)
    pgf = at("pgf", TAIL + 3840, [P, 4, NB])
    pgr = at("pgr", TAIL + 3968, [P, 4 * NB], U32)
    kitok = at("kitok", A3 + 68672, [P, 4, P])
    kistok = at("kistok", A3 + 70720, [NB, P])
    prob = accS
    probT = reluP
    qT = qiT[0]
    vcur = at("vcur", A3 + 26752, [P, 4, P])
    pool_hi = at("pool_hi", A2, [P, 8, TOK], F32R)
    pool_lo = at("pool_lo", A2 + 16640, [P, 8, TOK], F32R)
    big1 = at("big1", A2, [P, KT, TOK])
    big2 = at("big2", A2 + 33280, [P, KT, TOK])
    Z0 = A2 + 33280
    wpool = at("wpool", Z0, [P, 4, 2, 256])
    state = at("state", Z0 + 8192, [NB * STATE, PW])
    ub = [at(f"ub{p}", Z0 + 12288 + 2112 * p, [P, 16 + SEQ]) for p in range(2)]
    ext = [at(f"ext{p}", Z0 + 16512 + 512 * p, [P, NB, 16]) for p in range(2)]
    win = [at(f"win{p}", Z0 + 17536 + 2112 * p, [P, 16 + SEQ]) for p in range(2)]
    pooled = at("pooled", Z0 + 21760, [P, 2, TOK])
    pstage = at("pstage", Z0 + 25920, [STATE, 256])
    sstage = at("sstage", Z0 + 26944, [NB, 256])
    wsum8 = at("wsum8", Z0 + 27968, [P, NB])
    Z = A2 + 66560
    e_back = at("e_back", Z, [P, TOK])
    s_back = at("s_back", Z + 2080, [P, TOK])
    idxS = at("idxS", Z + 4160, [NB, TOPK_S], U32)
    idx8 = at("idx8", Z + 5184, [NB, 8], U32)
    ksel = at("ksel", A2, [P, 2, 512])
    vsel = at("vsel", A2 + 4096, [P, 2, 512])
    kselT = at("kselT", A2 + 8192, [P, KVH, 256])
    pS = at("pS", A2 + 12288, [HEADS, 256])
    pST = at("pST", A2 + 13312, [P, 2, HEADS])
    rowf = at("rowf", A2 + 13440, [NB, 6, 256])
    rowT = at("rowT", A2 + 19584, [P, 2, NB], U32)
    ptf = at("ptf", A2 + 19648, [NB, PAGES])
    pti = at("pti", A2 + 19712, [NB, PAGES], I32)
    att_stage = [at(f"att_stage{s}", Z + 2048 * s, [P, SEQ]) for s in range(4)]
    yrow = at("yrow", A2, [P, 4, D])
    sm = at("sm", Z, [P, KT, P], F32R)
    gate_p = at("gate_p", A2 + 33280, [P, D])
    gate_s = at("gate_s", A2 + 41472, [NB, D])
    gfin = at("gfin", A2 + 49664, [P, D])
    xch = at("xch", A2 + 57856, [P, 4, 512])
    srow = at("srow", A0 + 2816, [2 * NB, 512])

    bT = misc[:, 0:48]
    gT = misc[:, 48:64]
    spT = misc[:, 64:72]
    ss = misc[:, 72:80]
    rstd = misc[:, 80:88]
    mxq = misc[:, 88:92]
    nmq = misc[:, 92:96]
    sumq = misc[:, 96:100]
    rq = misc[:, 100:104]
    wiq = misc[:, 104:152]
    rcnt = misc[:, 152:216]
    sel8 = misc[0:16, 414:478]
    cT = misc[:, 240:384].rearrange("p (t b) -> p t b", b=9)
    max8 = misc[:, 392:400]
    eps = misc[:, 400:401]
    lane = misc[:, 403:404]
    vS = misc[:, 480:512].rearrange("p (k b) -> p k b", b=NB)

    acc = [ctx.enter_context(nc.psum_tensor(f"acc{p}", [P, 2, 512], F32)) for p in range(2)]
    ps = ctx.enter_context(nc.psum_tensor("ps", [P, 4, 512], F32))
    accv = [a[:, :, 0:HALF] for a in acc]
    modT = [acc[g % 2][:, 1, 128:200].rearrange("p (m t b) -> p m t b", m=2, b=9) for g in range(4)]
    xsT = acc[0][:, 1, 0:128].rearrange("p (t b) -> p t b", b=NB)

    att_dram = nc.dram_tensor("att_dram", (HEADS, P, SEQ), F32).ap()
    gate_dram = nc.dram_tensor("gate_dram", (NB + 1, D), F32).ap()

    raw_landed = [sem(f"raw_landed{p}") for p in range(2)]
    ring_landed = [sem(f"ring_landed{i}") for i in range(RING)]
    hi_ready = [sem(f"hi_ready{p}") for p in range(2)]
    lo_ready = [sem(f"lo_ready{p}") for p in range(2)]
    unit_done = [sem(f"unit_done{p}") for p in range(2)]
    acc_free = [sem(f"acc_free{p}") for p in range(2)]
    S = sem

    w_in, w_ada, w_a, w_b, w_out = (t[n][0] for n in ("w_in", "w_ada", "w_a_proj", "w_b_proj", "w_out"))

    def cols(w, c):
        return w[:, bass.ds(c, P)].rearrange("(k p) n -> p k n", p=P)

    def quarter(w, kq, c):
        return w[kq * 512:(kq + 1) * 512, bass.ds(c, 512)].rearrange("(k p) n -> p k n", p=P)

    def halves(ap):
        return ap.rearrange("p (a n) -> p a n", a=2)

    block = ctx.enter_context(nc.Block())

    @block.sync
    def _(sp):
        def load(q, p, src, first=False):
            if not first:
                sp.wait_ge(lo_ready[p], q)
            k, n = src.shape[1], src.shape[2]
            dst = raw[p][:, 0:k * n].rearrange("p (k n) -> p k n", n=n)
            sp.dma_start(dst, src).then_inc(raw_landed[p], 16)

        for dst, src in ((rows_cs[:], t["c_sample"].rearrange("b (t p) -> (b t) p", p=P)),
                         (rows_cp[:], t["c_prompt"].rearrange("b (t p) -> (b t) p", p=P)),
                         (rows_b[:], t["b_ada"].rearrange("b (t p) -> (b t) p", p=P)),
                         (rows_gs[0:16, :], t["g_norm"].rearrange("b (t p) -> (b t) p", p=P)),
                         (rows_gs[16:24, :], t["s_pool"].rearrange("b (t p) -> (b t) p", p=P)),
                         (ident[:], t["k_ident"]), (sel8, t["k_sel"]),
                         (rcnt, t["k_rcnt"]), (tri[:], t["k_tri"]), (lane, t["k_lane"])):
            sp.dma_start(dst, src).then_inc(S("tables_landed"), 16)
        sp.dma_start(pgi[:], t["page_table"].rearrange("(o b) n -> o b n", o=1).broadcast_to([P, NB, PAGES])
                     ).then_inc(S("pages_landed"), 16)
        sp.dma_start(gate_bias[:], t["b_ada"][0:1, 2 * D:3 * D].broadcast_to([NB + 1, D])
                     ).then_inc(S("gate_bias_landed"), 16)
        for u in range(ADA_UNITS):
            if u >= RING:
                sp.wait_ge(S("ring_done"), u - RING + 1)
            sp.dma_start(ring[u % RING][:].rearrange("p (k n) -> p k n", n=512),
                         quarter(w_ada, u % 4, 512 * ADA_CHUNKS[u // 4])).then_inc(ring_landed[u % RING], 16)
            if u == 1:
                sp.dma_start(xs[:], t["x_sample"].rearrange("b s d -> (b s) d")).then_inc(S("xs_landed"), 16)
            if 2 <= u < 6:
                i = u - 2
                sp.dma_start(x_tok[:, i, :], t["x_prompt"][0, i * P:(i + 1) * P, :]).then_inc(S(f"x_landed{i}"), 16)
            if u == 24:
                sp.wait_ge(S("gate_rows_ready"), 4)
                sp.dma_start(gate_dram, gate_rows[:]).then_inc(S("gate_stored"), 16)
        sp.wait_ge(S("ring_done"), ADA_UNITS - RING + 1)
        load(Q_A, 0, cols(w_in, C_WI), first=True)
        sp.wait_ge(S("ring_done"), ADA_UNITS - RING + 2)
        load(Q_A, 1, cols(w_in, C_KI), first=True)
        sp.wait_ge(S("xT_act"), 4)
        sp.dma_start(cosT[:], t["k_cos"]).then_inc(S("rope_landed"), 16)
        sp.dma_start(sinT[:], t["k_sin"]).then_inc(S("rope_landed"), 16)
        with sp.Fori(0, 8) as i:
            load(Q_A + 1 + i, 0, cols(w_in, C_QI + 256 * i))
            load(Q_A + 1 + i, 1, cols(w_in, C_QI + P + 256 * i))
        for j in range(8):
            load(Q_B + j // 2, j % 2, cols(w_in, C_K + P * j))
        sp.wait_ge(S("ki_tok_ready"), 1)
        sp.dma_start(out["kidx_p"].rearrange("(t p) d -> p t d", p=P), kitok[:]).then_inc(S("out_front"), 16)
        sp.dma_start(out["kidx_s"], kistok[:]).then_inc(S("out_front"), 16)
        load(Q_C, 0, cols(w_in, C_Q))
        load(Q_C, 1, cols(w_in, C_GA))
        sp.wait_ge(S("kv_evac"), 8)
        sp.dma_start(out["k_p"].rearrange("(t p) d -> p t d", p=P), ktok[:]).then_inc(S("out_front"), 16)
        sp.dma_start(out["v_p"].rearrange("(t p) d -> p t d", p=P), vtok[:]).then_inc(S("out_front"), 16)
        sp.wait_ge(S("stok_ready"), 1)
        sp.dma_start(out["k_s"], stok[:, 0, :]).then_inc(S("out_front"), 16)
        sp.dma_start(out["v_s"], stok[:, 1, :]).then_inc(S("out_front"), 16)
        with sp.Fori(1, HEADS) as h:
            load(Q_C + h, 0, cols(w_in, C_Q + P * h))
            load(Q_C + h, 1, cols(w_in, C_GA + P * h))
        load(Q_D, 0, cols(w_in, C_U))
        load(Q_D, 1, cols(w_in, C_U + P))
        sp.wait_ge(S("att_stored"), HEADS * 16)
        sp.wait_ge(S("front_done"), 1)
        sp.dma_start(wpool[:], t["w_pool"][0].rearrange("g (c p) d -> p g c d", p=P)).then_inc(S("pool_landed"), 16)
        sp.dma_start(state[:], t["state_pool"][0].rearrange("b s c -> (b s) c")).then_inc(S("pool_landed"), 16)
        sp.dma_start(out["pool_s"][:, 0:STATE - 1, :], t["state_pool"][0, :, 1:STATE, :]).then_inc(S("out_pool"), 16)
        for g in range(4):
            if g:
                load(Q_D + 2 * g, 0, cols(w_in, C_U + 256 * g))
                load(Q_D + 2 * g, 1, cols(w_in, C_U + 256 * g + P))
            load(Q_D + 2 * g + 1, 0, cols(w_in, C_GB + 256 * g))
            load(Q_D + 2 * g + 1, 1, cols(w_in, C_GB + 256 * g + P))
            sp.wait_ge(S("u_tok_ready"), 2 * g + 2)
            sp.dma_start(out["pool_p"][:, 256 * g:256 * g + 256], pstage[:]).then_inc(S("out_pool"), 16)
            sp.dma_start(out["pool_s"][:, STATE - 1, 256 * g:256 * g + 256], sstage[:]).then_inc(S("out_pool"), 16)
        sp.wait_ge(S("out_pool"), 9 * 16)
        with sp.Fori(Q_E, Q_F1) as q:
            load(q, 0, cols(w_in, P * q + (C_MB - P * Q_E)))
            load(q, 1, cols(w_b, P * q - P * Q_E))
        load(Q_F1, 0, cols(w_in, C_MA))
        load(Q_F1, 1, cols(w_in, C_MA + P))
        sp.wait_ge(unit_done[1], Q_F1)
        sp.dma_start(pti[:], t["page_table"]).then_inc(S("pt_landed"), 16)
        for b in range(NB):
            if b:
                sp.wait_ge(S("sa_pv"), b)
            for dst, src in ((ksel, out["k_s"]), (vsel, out["v_s"])):
                for hf in range(2):
                    sp.dma_start(dst[:, hf, :], src[b:b + 1, :].broadcast_to([P, 512])).then_inc(S("sa_new"), 16)
        with sp.Fori(1, 8) as i:
            load(Q_F1 + i, 0, cols(w_in, C_MA + 256 * i))
            load(Q_F1 + i, 1, cols(w_in, C_MA + 256 * i + P))
        load(Q_F2, 0, cols(w_a, 0))
        load(Q_F2, 1, cols(w_a, P))
        sp.wait_ge(S("sma_ready"), 16)
        for k in range(KT):
            if k >= 4:
                sp.wait_ge(S("att_split"), k - 3)
            sp.dma_start(att_stage[k % 4][:], att_dram[k]).then_inc(S(f"att_landed{k % 4}"), 16)
        with sp.Fori(1, 8) as i:
            load(Q_F2 + i, 0, cols(w_a, 256 * i))
            load(Q_F2 + i, 1, cols(w_a, 256 * i + P))
        sp.dma_start(ys[:], t["x_sample"].rearrange("b s d -> (b s) d")).then_inc(S("xs2_landed"), 16)
        for kq in range(2):
            load(Q_G, kq, quarter(w_out, kq, 0))
        sp.wait_ge(S("sm_ready"), 1)
        sp.dma_start(gate_p[:], gate_dram[0:1, :].broadcast_to([P, D])).then_inc(S("g_landed"), 16)
        sp.dma_start(gate_s[:], gate_dram[1:NB + 1, :]).then_inc(S("g_landed"), 16)
        sp.dma_start(gfin[:], t["g_final"].rearrange("(o d) -> o d", o=1).broadcast_to([P, D])
                     ).then_inc(S("g_landed"), 16)
        sp.dma_start(xch[:], t["x_prompt"][0, :, 0:512].rearrange("(t p) n -> p t n", p=P)
                     ).then_inc(S("xch_landed"), 16)
        for kq in range(2, 4):
            load(Q_G + 1, kq - 2, quarter(w_out, kq, 0))
        with sp.Fori(1, 4) as c:
            for kq in range(4):
                load(Q_G + 2 * c + kq // 2, kq % 2, quarter(w_out, kq, 512 * c))
            sp.wait_ge(S("y_added"), 4 * c)
            sp.dma_start(xch[:], t["x_prompt"][0, :, bass.ds(512 * c, 512)].rearrange("(t p) n -> p t n", p=P)
                         ).then_inc(S("xch_landed"), 16)
        for i in range(4):
            sp.wait_ge(S("y_ready"), i + 1)
            sp.dma_start(out["y_p"][i * P:(i + 1) * P, :], yrow[:, i, :]).then_inc(S("out_y"), 16)
        sp.wait_ge(S("y_ready"), 5)
        sp.dma_start(out["y_s"], ys[:]).then_inc(S("out_y"), 16)
        sp.wait_ge(S("out_y"), 5 * 16)

    @block.gpsimd
    def _(pool):
        def lo(q, p):
            pool.wait_ge(hi_ready[p], q + 1)
            nc.gpsimd.tensor_tensor(wlo[p][:], raw[p][:], whi[p][:].bitcast(F32), ALU.subtract).then_inc(lo_ready[p], 1)

        pool.wait_ge(S("ring_done"), ADA_UNITS)
        lo(Q_A, 0)
        lo(Q_A, 1)
        with pool.Fori(Q_A + 1, Q_B + 1) as q:
            lo(q, 0)
            lo(q, 1)
        kx = t["cache_kidx"][0].rearrange("n (g r) d -> (n g) (r d)", r=4)

        def gather(u):
            if u >= 3:
                pool.wait_ge(S("si_T"), u - 2)
            nc.gpsimd.indirect_dma_start(
                kib[u % 3][:], None, kx, bass.IndirectOffsetOnAxis(ap=pgr[:, u:u + 1], axis=0),
                bounds_check=kx.shape[0] - 1, oob_is_err=False).then_inc(S(f"kib_landed{u % 3}"), 16)

        pool.wait_ge(S("pgr_ready"), 1)
        pool.wait_ge(S("act_lo_ready"), KT)
        for u in range(3):
            gather(u)
        lo(Q_B + 1, 0)
        for j in range(1, 8):
            for u in range(4 * j - 1, 4 * j + 3):
                gather(u)
            lo(Q_B + (j + 2) // 2, j % 2)
        gather(CHUNKS - 1)

        def value_head(h):
            nc.gpsimd.tensor_copy(vcur[:], vtok[:, :, (h // 4) * P:(h // 4) * P + P] if isinstance(h, int) else
                                  vtok[:, :, bass.ds((h // 4) * P, P)]).then_inc(S("vcur_ready"), 1)

        pool.wait_ge(S("kv_evac"), 8)
        pool.wait_ge(S("si_hr"), CHUNKS + 1)
        value_head(0)
        with pool.Fori(1, HEADS) as h:
            lo(Q_C + h, 0)
            lo(Q_C + h, 1)
            pool.wait_ge(S("attn_pv"), h)
            value_head(h)
        with pool.Fori(Q_D, Q_F1) as q:
            lo(q, 0)
            lo(q, 1)
        lo(Q_F1, 0)
        lo(Q_F1, 1)
        kf = t["cache_k"][0].rearrange("n s h d -> (n s) (h d)")
        vf = t["cache_v"][0].rearrange("n s h d -> (n s) (h d)")
        pool.wait_ge(S("rows_ready"), 1)
        for b in range(NB):
            pool.wait_ge(S("sa_new"), 64 * (b + 1))
            for hf in range(2):
                for dst, src in ((ksel, kf), (vsel, vf)):
                    nc.gpsimd.indirect_dma_start(
                        dst[:, hf, :], None, src, bass.IndirectOffsetOnAxis(ap=rowT[:, hf, b:b + 1], axis=0),
                        bounds_check=src.shape[0] - 1, oob_is_err=False).then_inc(S("sa_sel"), 16)
        with pool.Fori(Q_F1 + 1, Q_G) as q:
            lo(q, 0)
            lo(q, 1)
        with pool.Fori(Q_G, Q_END) as q:
            lo(q, 0)

    @block.scalar
    def _(act):
        def hi(q, p, first=False):
            act.wait_ge(raw_landed[p], 16 * (q + 1))
            if not first:
                act.wait_ge(unit_done[p], q)
            nc.scalar.copy(whi[p][:], raw[p][:]).then_inc(hi_ready[p], 1)

        def root(n, i, summed, count):
            act.wait_ge(summed, count)
            nc.scalar.activation(rstd[0:n, i:i + 1], ss[0:n, i:i + 1], ACT.Sqrt, bias=eps[0:n, :],
                                 scale=1.0 / D).then_inc(S("root_ready"), 1)

        act.wait_ge(S("tables_landed"), 10 * 16)
        nc.scalar.copy(identb[:], ident[:]).then_inc(S("identb_ready"), 1)

        def squares(i):
            n, x = (P, x_tok[:, i, :]) if i < 4 else (NB, xs[:])
            act.wait_ge(S(f"x_landed{i}") if i < 4 else S("xs_landed"), 16)
            done = 0 if i == 4 else i + 1
            if done:
                act.wait_ge(S("ss_ready"), done)
            nc.scalar.activation(square_dump[0:n, :], x, ACT.Square, accum_out=ss[0:n, i:i + 1]
                                 ).then_inc(S("ss_ready"), 1)
            if i == 4:
                act.wait_ge(S("eps_ready"), 1)
            root(n, i, S("ss_ready"), done + 1)

        def x_columns(i):
            act.wait_ge(S("xT_done"), i + 1)
            for j in range(2):
                last = nc.scalar.copy(H[:, 4 * j:4 * j + 4, i * P:(i + 1) * P],
                                      ps[:, j, :].rearrange("p (k n) -> p k n", n=P))
            last.then_inc(S("xT_act"), 1)

        def mod_rows(c):
            act.wait_ge(S("ring_done"), 4 * (c + 1))
            if c >= 6:
                act.wait_ge(S("mod_T"), c - 5)
            nc.scalar.copy(modb[c % 2][:], acc[c % 2][0:NB + 1, 0, :]).then_inc(S("mod_rows"), 1)

        def act_high(g):
            for k in range(4 * g, 4 * g + 4):
                act.wait_ge(S("H_ready"), k + 1)
                nc.scalar.copy(act_hi[:, k, :], H[:, k, :]).then_inc(S("act_hi_ready"), 1)

        squares(4)
        squares(0)
        squares(1)
        x_columns(0)
        squares(2)
        x_columns(1)
        squares(3)
        x_columns(2)
        mod_rows(4)
        x_columns(3)
        mod_rows(5)
        act.wait_ge(S("gate_stored"), 16)
        for g in range(1, 4):
            mod_rows(4 + 2 * g)
            mod_rows(5 + 2 * g)
            act_high(g - 1)
        act.wait_ge(S("ring_done"), ADA_UNITS)
        hi(Q_A, 0, first=True)
        hi(Q_A, 1, first=True)
        act_high(3)

        def relu_scores(h, first=False):
            act.wait_ge(S("idx_mm"), h + 1)
            if not first:
                act.wait_ge(S("idx_acc"), h)
            for b in (1, 2, 3):
                w = (b + 1) * P
                last = nc.scalar.activation(reluP[:, OFF[b]:OFF[b] + w], ps[:, b - 1, 0:w], ACT.Relu)
            last.then_inc(S("idx_relu"), 1)

        hi(Q_A + 1, 0)
        hi(Q_A + 1, 1)
        hi(Q_A + 2, 0)
        hi(Q_A + 2, 1)
        relu_scores(0, first=True)
        with act.Fori(1, 8) as i:
            hi(Q_A + 2 + i, 0)
            relu_scores(2 * i - 1)
            hi(Q_A + 2 + i, 1)
            relu_scores(2 * i)
        def chunk_keys(u):
            act.wait_ge(S("si_T"), u + 1)
            if u >= 2:
                act.wait_ge(S("si_qk"), u - 1)
            nc.scalar.copy(kiTc[u % 2][:].rearrange("p (c r) -> p r c", r=4),
                           ps[:, 2, :].rearrange("p (r c) -> p r c", r=4)).then_inc(S("si_ka"), 1)

        def chunk_relu(u, n=512):
            act.wait_ge(S("si_qk"), u + 1)
            if u >= 2:
                act.wait_ge(S("si_hr"), u - 1)
            nc.scalar.activation(reluS[u % 2][:, 0:n], ps[0:HEADS, 3, 0:n], ACT.Relu).then_inc(S("si_relu"), 1)

        def chunks_of_tile(j):
            for u in range(4 * j - 4, 4 * j):
                if u:
                    chunk_relu(u - 1)
                chunk_keys(u)

        relu_scores(15)
        hi(Q_B + 1, 0)
        act.wait_ge(S("idx_acc"), HEADS)
        for j in range(1, 8):
            chunks_of_tile(j)
            hi(Q_B + 1 + j // 2, j % 2)
        chunks_of_tile(8)
        chunk_relu(CHUNKS - 1)
        chunk_relu(CHUNKS, n=NB)

        def body_c(h, first=False):
            q = Q_C + h
            hi(q + 1, 0)
            if not first:
                act.wait_ge(S("attn_T"), h)
                nc.scalar.copy(probT[:, 0:512], ps[:, 0, :]).then_inc(S("pt_act"), 1)
            hi(q + 1, 1)
            act.wait_ge(unit_done[1], q + 1)
            if not first:
                act.wait_ge(S("sga_ready"), h)
            nc.scalar.activation(halves(ebuf[:]), accv[1], ACT.Exp, scale=-1.0).then_inc(S("ega_ready"), 1)
            act.wait_ge(S("nm_ready"), h + 1)
            for b in range(4):
                bank, c = S_AT[b]
                w = (b + 1) * P
                last = nc.scalar.activation(prob[:, OFF[b]:OFF[b] + w], ps[:, bank, c:c + w], ACT.Exp,
                                            bias=nmq[:, b:b + 1], scale=ATT_SCALE, accum_out=sumq[:, b:b + 1])
            last.then_inc(S("exp_done"), 1)
            if not first:
                act.wait_ge(S("attn_evac"), h)
                act.dma_start(att_dram[bass.ds(h - 1, 1)].rearrange("o p n -> (o p) n"), silu_ga[:, h - 1, 0:SEQ]
                              ).then_inc(S("att_stored"), 16)

        body_c(0, first=True)
        with act.Fori(1, HEADS) as h:
            body_c(h)
        act.wait_ge(S("attn_T"), HEADS)
        nc.scalar.copy(probT[:, 0:512], ps[:, 0, :]).then_inc(S("pt_act"), 1)
        act.wait_ge(S("attn_evac"), HEADS)
        act.dma_start(att_dram[HEADS - 1], silu_ga[:, HEADS - 1, 0:SEQ]).then_inc(S("att_stored"), 16)
        act.wait_ge(S("att_stored"), HEADS * 16)
        act.wait_ge(S("front_done"), 1)
        for g in range(4):
            q = Q_D + 2 * g
            hi(q + 1, 0)
            hi(q + 1, 1)
            for j in range(2):
                hi(q + 2, j)
                if g or j:
                    act.wait_ge(S("pg_ready"), 2 * g + j)
                nc.scalar.activation(halves(e_back[:]), accv[j], ACT.Exp, scale=-1.0).then_inc(S("egb_ready"), 1)
                act.wait_ge(S("pg_ready"), 2 * g + j + 1)
                nc.scalar.copy(pool_hi[:, 2 * g + j, :], s_back[:]).then_inc(S("pool_hi_ready"), 1)
        act.wait_ge(S("pg_ready"), 8)
        with act.Fori(0, KT) as j:
            q = Q_E + j
            hi(q + 1, 0)
            act.wait_ge(S("smb_ready"), j)
            nc.scalar.activation(halves(e_back[:]), accv[0], ACT.Exp, scale=-1.0).then_inc(acc_free[0], 1)
            hi(q + 1, 1)
        act.wait_ge(S("smb_ready"), KT)
        for b in range(NB):
            act.wait_ge(S("sa_T"), b + 1)
            nc.scalar.copy(kselT[:, 0:2, :].rearrange("p a n -> p (a n)"), ps[:, 0, :]).then_inc(S("sa_ka"), 1)
            act.wait_ge(S("sa_nm"), b + 1)
            nc.scalar.activation(pS[:], ps[0:HEADS, 2, 0:256], ACT.Exp, bias=nmq[0:HEADS, 0:1], scale=ATT_SCALE,
                                 accum_out=sumq[0:HEADS, 0:1]).then_inc(S("sa_exp"), 1)
        with act.Fori(0, 8) as i:
            q = Q_F1 + i
            for p in range(2):
                hi(q + 1, p)
                act.wait_ge(S("sma_ready"), 2 * i + p)
                nc.scalar.activation(halves(e_back[:]), accv[p], ACT.Exp, scale=-1.0).then_inc(acc_free[p], 1)
        for k in range(KT):
            act.wait_ge(S(f"att_landed{k % 4}"), 16 * (k // 4 + 1))
            if k == 0:
                act.wait_ge(S("attS_ready"), NB)
            nc.scalar.copy(act_hi[:, k, 0:SEQ], att_stage[k % 4][:])
            nc.scalar.copy(act_hi[:, k, SEQ:TOK], attS[:, k, :]).then_inc(S("att_hi_ready"), 1)
        with act.Fori(Q_F2, Q_G) as q:
            hi(q + 1, 0)
            hi(q + 1, 1)
        for k in range(KT):
            act.wait_ge(S("m_ready"), k + 1)
            nc.scalar.copy(act_hi[:, k, :], big2[:, k, :]).then_inc(S("m_hi_ready"), 1)
        act.wait_ge(S("sm_zero"), 1)
        nc.scalar.copy(sm[:, :, 0:NB], big2[:, :, SEQ:TOK]).then_inc(S("sm_hi_ready"), 1)
        with act.Fori(Q_G, Q_END - 1) as q:
            hi(q + 1, 0)
            hi(q + 1, 1)
        for i in range(5):
            act.wait_ge(S("y_all"), 1)
            if i:
                act.wait_ge(S("ssy_ready"), i)
            src = yrow[:, i, :] if i < 4 else ys[:]
            n = P if i < 4 else NB
            nc.scalar.activation(xch[0:n].rearrange("p a n -> p (a n)"), src, ACT.Square,
                                 accum_out=ss[0:n, i:i + 1]).then_inc(S("ssy_ready"), 1)
            root(n, i, S("ssy_ready"), i + 1)

    @block.vector
    def _(dve):
        v = nc.vector
        chain = Chain(dve, sem("dve_chain"))
        step = chain.step

        def lo(q, p):
            dve.wait_ge(hi_ready[p], q + 1)
            v.tensor_tensor(wlo[p][:], raw[p][:], whi[p][:].bitcast(F32), ALU.subtract).then_inc(lo_ready[p], 1)

        def inverse_root(n, i, count):
            dve.wait_ge(S("root_ready"), count)
            step(v.reciprocal(rstd[0:n, i:i + 1], rstd[0:n, i:i + 1]))

        v.memset(eps, EPS).then_inc(S("eps_ready"), 1)
        dve.wait_ge(S("pages_landed"), 16)
        dve.wait_ge(S("tables_landed"), 10 * 16)
        for i in range(4):
            g = slice(32 * i, 32 * i + 32)
            last = v.tensor_copy(pgf[g], pgi[g, :, i::4].rearrange("p b n -> p n b"))
        step(last)
        pg = pgf[:].rearrange("p n b -> p (n b)")
        step(v.scalar_tensor_tensor(pg, pg, 32.0, lane.broadcast_to([P, 4 * NB]), ALU.mult, ALU.add))
        v.tensor_copy(pgr[:], pg).then_inc(S("pgr_ready"), 1)
        dve.wait_ge(S("rows_T"), 1)
        v.tensor_copy(cT[:, :, 1:9], ps[:, 0, 0:128].rearrange("p (b t) -> p t b", b=NB))
        v.tensor_copy(bT, ps[:, 1, 16:64])
        v.tensor_copy(misc[:, 48:72], ps[:, 1, 64:88])
        v.tensor_copy(cT[:, :, 0], ps[:, 1, 0:16]).then_inc(S("cT_ready"), 1)
        inverse_root(NB, 4, 1)
        v.tensor_scalar(xs[:], xs[:], rstd[0:NB, 4:5], None, ALU.mult).then_inc(S("xs_ready"), 1)

        def x_hat(i):
            inverse_root(P, i, i + 2)
            v.tensor_scalar(x_tok[:, i, :], x_tok[:, i, :], rstd[:, i:i + 1], None, ALU.mult
                            ).then_inc(S("xhat_ready"), 1)

        def x_columns(i):
            dve.wait_ge(S("xT_done"), i + 1)
            for j in range(2, 4):
                last = v.tensor_copy(H[:, 4 * j:4 * j + 4, i * P:(i + 1) * P],
                                     ps[:, j, :].rearrange("p (k n) -> p k n", n=P))
            last.then_inc(S("xT_dve"), 1)

        def gate_row(c):
            dve.wait_ge(S("ring_done"), 4 * (c + 1))
            v.tensor_tensor(gate_rows[:, 512 * c:512 * (c + 1)], acc[c % 2][0:NB + 1, 0, :],
                            gate_bias[:, 512 * c:512 * (c + 1)], ALU.add).then_inc(S("gate_rows_ready"), 1)

        dve.wait_ge(S("gate_bias_landed"), 16)
        x_hat(0)
        gate_row(0)
        dve.wait_ge(S("xs_T"), 1)
        step(v.tensor_copy(H[:, :, SEQ:TOK], xsT))
        for i in range(1, 4):
            x_hat(i)
            gate_row(i)
            x_columns(i - 1)
        x_columns(3)
        dve.wait_ge(S("xT_act"), 4)
        dve.wait_ge(S("xT_dve"), 4)

        def act_low(k):
            dve.wait_ge(S("act_hi_ready"), k + 1)
            v.tensor_tensor(act_lo[:, k, :], H[:, k, :], act_hi[:, k, :].bitcast(F32), ALU.subtract
                            ).then_inc(S("act_lo_ready"), 1)

        def modulate(g):
            def per_tok(a):
                return a[:, 4 * g:4 * g + 4].unsqueeze(2).broadcast_to([P, 4, 9])

            ks = slice(4 * g, 4 * g + 4)
            dve.wait_ge(S("mod_T"), 2 * g + 2)
            v.tensor_tensor(mB[:, ks, :], modT[g][:, 0], per_tok(bT[:, 0:16]), ALU.add)
            step(v.tensor_tensor(mA[:, ks, :], modT[g][:, 1], per_tok(bT[:, 16:32]), ALU.add))
            step(v.scalar_tensor_tensor(mA[:, ks, :], mA[:, ks, :], 1.0, per_tok(gT), ALU.add, ALU.mult))
            step(v.tensor_tensor(H[:, ks, SEQ:TOK], H[:, ks, SEQ:TOK], mA[:, ks, 1:9], ALU.mult))
            step(v.tensor_tensor(H[:, ks, SEQ:TOK], H[:, ks, SEQ:TOK], mB[:, ks, 1:9], ALU.add))
            for k in range(4 * g, 4 * g + 4):
                v.tensor_scalar(H[:, k, 0:SEQ], H[:, k, 0:SEQ], mA[:, k, 0:1], mB[:, k, 0:1], ALU.mult, ALU.add
                                ).then_inc(S("H_ready"), 1)
                if g == 3:
                    act_low(k - 4)

        modulate(0)
        for g in range(1, 4):
            modulate(g)
            if g < 3:
                for k in range(4 * g - 4, 4 * g):
                    act_low(k)
        for k in range(12, 16):
            act_low(k)

        def rope(q, p, fills, dst, ready, ready_n):
            dve.wait_ge(unit_done[p], q + 1)
            v.tensor_tensor(halves(dst), accv[p], halves(cosT[:]), ALU.mult)
            v.tensor_tensor(halves(swp[0:64, :]), accv[p][64:128], halves(sinT[64:128, :]), ALU.mult)
            v.tensor_tensor(halves(swp[64:128, :]), accv[p][0:64], halves(sinT[0:64, :]), ALU.mult
                            ).then_inc(acc_free[p], 1)
            dve.wait_ge(acc_free[p], fills + 1)
            v.tensor_tensor(dst, dst, swp[:], ALU.add).then_inc(ready, 1)
            dve.wait_ge(ready, ready_n)

        dve.wait_ge(unit_done[0], Q_A + 1)
        v.tensor_scalar(halves(wiT[:]), accv[0][0:HEADS], IDX_SCALE, None, ALU.mult).then_inc(acc_free[0], 1)
        dve.wait_ge(S("rope_landed"), 32)
        rope(Q_A, 1, N_A, kiT[:], S("ki_ready"), 1)
        step(v.memset(accS[:, P:1280], 0.0))
        for b in (1, 2, 3):
            last = v.tensor_scalar(accS[:, OFF[b] + b * P:OFF[b] + (b + 1) * P], tri[:], 1e8, None, ALU.mult)
        step(last)

        def add_scores(h, first=False):
            dve.wait_ge(S("idx_relu"), h + 1)
            if not first:
                dve.wait_ge(S("idx_acc"), h)
            for b in (1, 2, 3):
                a = accS[:, OFF[b]:OFF[b] + (b + 1) * P]
                last = v.scalar_tensor_tensor(a, reluP[:, OFF[b]:OFF[b] + (b + 1) * P],
                                              wiq[:, bass.ds((b - 1) * HEADS + h, 1)], a, ALU.mult, ALU.add)
            last.then_inc(S("idx_acc"), 1)

        def index_query(i, p, first=False):
            h = 2 * i + p
            if not first:
                dve.wait_ge(S("idx_mm"), h - 1)
            rope(Q_A + 1 + i, p, N_A + 1 + i, qiT[p][:], S("qi_ready"), h + 1)
            v.tensor_copy(qiS[:, :, bass.ds(h, 1)], qiT[p][:, SEQ:TOK].unsqueeze(2)).then_inc(S("qiS_done"), 1)

        index_query(0, 0, first=True)
        dve.wait_ge(S("ki_T"), 1)
        v.tensor_copy(wiq, ps[:, 3, 0:48])
        v.tensor_copy(kistok[:], ps[0:NB, 1, 0:P])
        v.tensor_copy(kitok[:].rearrange("p t d -> p (t d)"), ps[:, 0, :]).then_inc(S("ki_tok_ready"), 1)
        dve.wait_ge(S("ki_tok_ready"), 1)
        index_query(0, 1, first=True)
        add_scores(0, first=True)
        with dve.Fori(1, 8) as i:
            index_query(i, 0)
            add_scores(2 * i - 1)
            index_query(i, 1)
            add_scores(2 * i)
        rounds = [(b, r) for b in (1, 2, 3) for r in range(TOPK_P // 8)]

        def prompt_round(b):
            a = accS[:, OFF[b]:OFF[b] + (b + 1) * P]
            step(v.max(max8, a))
            step(v.match_replace(a, max8, a, TAKEN))

        def kv_rows(j):
            dve.wait_ge(S("kv_T"), j + 1)
            dst = ktok if j < 4 else vtok
            c = (j % 4) * P
            v.tensor_copy(dst[:, :, c:c + P], ps[:, 0, :].rearrange("p (t d) -> p t d", d=P)
                          ).then_inc(S("kv_evac"), 1)

        def sample_quarter(n):
            dve.wait_ge(S("si_hr"), 8 * n + 8)
            v.tensor_copy(scoreS[:, 512 * n:512 * n + 512], ps[0:NB, 1, :]).then_inc(S("si_q"), 1)

        for j in range(8):
            q, p = Q_B + j // 2, j % 2
            if j in (3, 5, 7):
                sample_quarter((j - 3) // 2)
            if j < 4:
                rope(q, p, N_B + j // 2, kT[:, j, :], S("kv_ready"), j + 1)
            else:
                dve.wait_ge(unit_done[p], q + 1)
                dve.wait_ge(S("kv_T"), j - 1)
                v.tensor_copy(vS[:, j - 4, :], acc[p][:, 1, SEQ - HALF:HALF])
                v.tensor_copy(halves(vT[p][:]), accv[p]).then_inc(S("kv_ready"), 1)
            if j == 0:
                add_scores(15)
                dve.wait_ge(S("idx_acc"), 16)
                step(v.memset(wiD[:], 0.0))
                v.tensor_copy(wiD[:].rearrange("h a b -> h (a b)")[:, 0:64:9], wiT[:, SEQ:TOK]).then_inc(S("wiD_ready"), 1)
            if j:
                kv_rows(j - 1)
            for b, _ in rounds[max(7 * j - 7, 0):7 * j]:
                prompt_round(b)
        kv_rows(7)
        v.tensor_copy(maskb[:, 0:P], tri[:])
        for b in (1, 2, 3):
            last = v.tensor_scalar(maskb[:, OFF[b]:OFF[b] + (b + 1) * P], accS[:, OFF[b]:OFF[b] + (b + 1) * P],
                                   -2e38, MASKED, ALU.is_gt, ALU.mult)
        last.then_inc(S("mask_ready"), 1)
        sample_quarter(3)
        dve.wait_ge(S("stok_T"), 1)
        v.tensor_copy(stok[:, 0, :], ps[0:NB, 0, :])
        v.tensor_copy(stok[:, 1, :], ps[0:NB, 2, :]).then_inc(S("stok_ready"), 1)
        dve.wait_ge(S("si_hr"), CHUNKS + 1)
        step(v.tensor_copy(scoreS[:, PAST:PAST + 1], ps[0:NB, 1, 0:1]))
        step(v.memset(qSm[:], 0.0))

        def evac(h, hp1):
            dve.wait_ge(S("attn_pv"), hp1)
            dve.wait_ge(S("sga_ready"), hp1)
            v.tensor_tensor(silu_ga[:, h, 0:SEQ], ps[:, 3, :], silu_ga[:, h, 0:SEQ], ALU.mult
                            ).then_inc(S("attn_evac"), 1)

        def pt_copy(hp1):
            dve.wait_ge(S("attn_T"), hp1)
            v.tensor_copy(probT[:, 512:1024], ps[:, 1, :])
            v.tensor_copy(probT[:, 1024:1280], ps[:, 2, 0:256]).then_inc(S("pt_dve"), 1)

        def body_c(h, first=False):
            q = Q_C + h
            rope(q, 0, N_C + h, qT[:], S("q_ready"), h + 1)
            kv = h // 4
            v.tensor_copy(qSm[:].rearrange("p b k h -> p b (k h)")[:, :, bass.ds(kv * HEADS + h, 1)],
                          qT[:, SEQ:TOK].unsqueeze(2))
            if not first:
                pt_copy(h)
            dve.wait_ge(S("ega_ready"), h + 1)
            step(v.tensor_scalar(ebuf[:], ebuf[:], 1.0, None, ALU.add))
            step(v.reciprocal(ebuf[:], ebuf[:]))
            if first:
                dve.wait_ge(S("out_front"), 6 * 16)
            v.tensor_tensor(halves(silu_ga[:, h, :]), accv[1], halves(ebuf[:]), ALU.mult).then_inc(acc_free[1], 1)
            dve.wait_ge(acc_free[1], N_C + h + 1)
            v.tensor_copy(sgaS[:, h, :], silu_ga[:, h, SEQ:TOK]).then_inc(S("sga_ready"), 1)
            if not first:
                evac(h - 1, h)
            dve.wait_ge(S("attn_qk"), h + 1)
            for b in range(4):
                bank, c = S_AT[b]
                last = v.reduce_max(mxq[:, b:b + 1], ps[:, bank, c:c + (b + 1) * P], AX.X)
            step(last)
            v.tensor_scalar(nmq, mxq, -ATT_SCALE, None, ALU.mult).then_inc(S("nm_ready"), 1)
            dve.wait_ge(S("exp_done"), h + 1)
            step(v.reciprocal(rq, sumq))
            for b in range(4):
                a = prob[:, OFF[b]:OFF[b] + (b + 1) * P]
                last = v.tensor_scalar(a, a, rq[:, b:b + 1], None, ALU.mult)
            last.then_inc(S("prob_ready"), 1)

        chain.enter(0, 0, 4)
        body_c(0, first=True)
        chain.leave(1)
        with dve.Fori(1, HEADS) as h:
            chain.enter(h, 1, 4)
            body_c(h)
        chain.leave(HEADS - 1)
        pt_copy(HEADS)
        evac(HEADS - 1, HEADS)
        dve.wait_ge(S("attn_evac"), HEADS)
        dve.wait_ge(S("att_stored"), HEADS * 16)
        v.memset(ub[0][:, 0:16], 0.0)
        v.memset(ub[1][:, 0:16], 0.0).then_inc(S("front_done"), 1)

        def sample_round(dst):
            a = scoreS[:, 0:PAST + 1]
            step(v.max(max8[0:NB], a))
            step(v.max_index(idx8[:], max8[0:NB], a))
            v.tensor_copy(dst, idx8[:])
            step(v.match_replace(a, max8[0:NB], a, TAKEN))

        dve.wait_ge(S("front_done"), 1)
        for g, w in enumerate(WINDOWS):
            for p in range(2):
                j = 2 * g + p
                dve.wait_ge(unit_done[p], Q_D + 2 * g + 1)
                if j >= 2:
                    dve.wait_ge(S("u_T"), j - 1)
                v.tensor_copy(ub[p][:, 16:16 + HALF], acc[p][:, 0, 0:HALF])
                v.tensor_copy(ub[p][:, 16 + HALF:16 + SEQ], acc[p][:, 1, 0:SEQ - HALF])
                v.tensor_copy(ext[p][:, :, 15:16], acc[p][:, 1, SEQ - HALF:HALF].unsqueeze(2)).then_inc(acc_free[p], 1)
                dve.wait_ge(S("state_T"), j + 1)
                v.tensor_copy(ext[p][:, :, 0:STATE],
                              ps[:, p, 0:NB * STATE].rearrange("p (b s) -> p b s", s=STATE)).then_inc(S("u_ready"), 1)
                dve.wait_ge(S("u_ready"), j + 1)
                src, s = ub[p], 1
                n = 0
                while s < w:
                    step(v.tensor_tensor(win[n % 2][:, 2 * s - 1:], src[:, 2 * s - 1:], src[:, s - 1:16 + SEQ - s],
                                         ALU.add))
                    src, s, n = win[n % 2], 2 * s, n + 1
                if j >= 2:
                    dve.wait_ge(S("mix_mm"), 2 * g)
                r = win[n % 2]
                step(v.tensor_tensor(r[:, 0:16], src[:, 16:32], rcnt[:, 16 * g:16 * g + 16], ALU.mult))
                v.tensor_tensor(pooled[:, p, 0:16], r[:, 0:16], ub[p][:, 16:32], ALU.subtract)
                v.scalar_tensor_tensor(pooled[:, p, 16:SEQ], src[:, 32:16 + SEQ], 1.0 / w, ub[p][:, 32:16 + SEQ],
                                       ALU.mult, ALU.subtract)
                step(v.tensor_reduce(wsum8[:], ext[p][:, :, 16 - w:16], AX.X, ALU.add))
                v.scalar_tensor_tensor(pooled[:, p, SEQ:TOK], wsum8[:], 1.0 / w, ext[p][:, :, 15], ALU.mult,
                                       ALU.subtract).then_inc(S("pooled_ready"), 1)
                if j >= 2 and p == 0:
                    dve.wait_ge(S("out_pool"), 16 * (2 * g + 1))
                dve.wait_ge(S("u_T"), j + 1)
                v.tensor_copy(pstage[:, p * P:(p + 1) * P], ps[0:STATE, p, 128:256])
                v.tensor_copy(sstage[:, p * P:(p + 1) * P], ps[0:NB, p, 256:384]).then_inc(S("u_tok_ready"), 1)
                sample_round(idxS[:, 8 * (4 * g + p):8 * (4 * g + p) + 8])
            for p in range(2):
                j = 2 * g + p
                dve.wait_ge(S("egb_ready"), j + 1)
                step(v.tensor_scalar(e_back[:], e_back[:], 1.0, None, ALU.add))
                step(v.reciprocal(e_back[:], e_back[:]))
                if j:
                    dve.wait_ge(S("pool_hi_ready"), j)
                v.tensor_tensor(halves(e_back[:]), accv[p], halves(e_back[:]), ALU.mult).then_inc(acc_free[p], 1)
                dve.wait_ge(acc_free[p], N_D + 2 * g + 2)
                dve.wait_ge(S("mix_mm"), j + 1)
                v.scalar_tensor_tensor(halves(s_back[:]), ps[:, 2:4, 0:HALF], spT[:, j:j + 1], halves(e_back[:]),
                                       ALU.mult, ALU.mult).then_inc(S("pg_ready"), 1)
                dve.wait_ge(S("pool_hi_ready"), j + 1)
                dve.wait_ge(S("pg_ready"), j + 1)
                v.tensor_tensor(pool_lo[:, j, :], s_back[:], pool_hi[:, j, :].bitcast(F32), ALU.subtract
                                ).then_inc(S("pool_ready"), 1)
                sample_round(idxS[:, 8 * (4 * g + 2 + p):8 * (4 * g + 2 + p) + 8])
        with dve.Fori(0, KT) as j:
            a = scoreS[:, 0:PAST + 1]
            chain.enter(j, 0, 5)
            step(v.max(max8[0:NB], a))
            dve.wait_ge(acc_free[0], N_E + j + 1)
            chain.count(v.tensor_scalar(e_back[:], e_back[:], 1.0, None, ALU.add))
            step(v.max_index(idx8[:], max8[0:NB], a))
            v.reciprocal(s_back[:], e_back[:]).then_inc(S("smb_ready"), 1)
            chain.count(v.tensor_copy(idxS[:, bass.ds(8 * j + 128, 8)], idx8[:]))
            step(v.match_replace(a, max8[0:NB], a, TAKEN))
            dve.wait_ge(S("smb_ready"), j + 1)
            dve.wait_ge(unit_done[1], Q_E + j + 1)
            v.tensor_tensor(halves(big2[:, j, :]), accv[1], halves(s_back[:]), ALU.mult).then_inc(acc_free[1], 1)
        chain.leave(KT)
        dve.wait_ge(unit_done[1], Q_F1)
        dve.wait_ge(S("pt_landed"), 16)
        r = [rowf[:, n, :] for n in range(6)]
        step(v.tensor_copy(ptf[:], pti[:]))
        step(v.tensor_copy(r[0], idxS[:]))
        v.tensor_scalar(r[3], r[0], float(PAST), 1e6, ALU.is_ge, ALU.mult)
        step(v.tensor_scalar(r[1].bitcast(U32), idxS[:], 7, None, ALU.logical_shift_right))
        step(v.tensor_copy(r[2], r[1].bitcast(U32)))
        step(v.scalar_tensor_tensor(r[3], r[2], -float(P), r[3], ALU.mult, ALU.add))
        step(v.tensor_tensor(r[3], r[3], r[0], ALU.add))
        for pg in range(PAGES):
            step(v.tensor_scalar(r[4], r[2], float(pg), ptf[:, pg:pg + 1], ALU.is_equal, ALU.mult))
            step(v.scalar_tensor_tensor(r[3], r[4], float(P), r[3], ALU.mult, ALU.add))
        v.tensor_copy(r[5], r[3]).then_inc(S("rowf_ready"), 1)
        dve.wait_ge(S("rowf_T"), 1)
        v.tensor_copy(rowT[:].rearrange("p a b -> p (a b)"), ps[:, 3, 0:2 * NB]).then_inc(S("rows_ready"), 1)
        for b in range(NB):
            dve.wait_ge(S("sa_T"), b + 1)
            v.tensor_copy(kselT[:, 2:4, :].rearrange("p a n -> p (a n)"), ps[:, 1, :]).then_inc(S("sa_kd"), 1)
            dve.wait_ge(S("sa_qk"), b + 1)
            step(v.reduce_max(mxq[0:HEADS, 0:1], ps[0:HEADS, 2, 0:256], AX.X))
            v.tensor_scalar(nmq[0:HEADS, 0:1], mxq[0:HEADS, 0:1], -ATT_SCALE, None, ALU.mult).then_inc(S("sa_nm"), 1)
            dve.wait_ge(S("sa_exp"), b + 1)
            step(v.reciprocal(rq[0:HEADS, 0:1], sumq[0:HEADS, 0:1]))
            v.tensor_scalar(pS[:], pS[:], rq[0:HEADS, 0:1], None, ALU.mult).then_inc(S("sa_prob"), 1)
            dve.wait_ge(S("sa_pT"), b + 1)
            v.tensor_copy(pST[:].rearrange("p a h -> p (a h)"), ps[:, 2, 256:256 + 2 * HEADS]).then_inc(S("sa_pst"), 1)
            dve.wait_ge(S("sa_pv"), b + 1)
            v.tensor_tensor(attS[:, :, b], ps[:, 3, 64:64 + HEADS], sgaS[:, :, b], ALU.mult).then_inc(S("attS_ready"), 1)
        with dve.Fori(0, 8) as i:
            chain.enter(i, 0, 2)
            for p in range(2):
                dve.wait_ge(acc_free[p], N_F1 + i + 1)
                step(v.tensor_scalar(e_back[:], e_back[:], 1.0, None, ALU.add))
                v.reciprocal(big1[:, 2 * i + p, :], e_back[:]).then_inc(S("sma_ready"), 1)
        chain.leave(8)
        for k in range(KT):
            dve.wait_ge(S("att_hi_ready"), k + 1)
            v.tensor_tensor(act_lo[:, k, 0:SEQ], att_stage[k % 4][:], act_hi[:, k, 0:SEQ].bitcast(F32), ALU.subtract)
            v.tensor_tensor(act_lo[:, k, SEQ:TOK], attS[:, k, :], act_hi[:, k, SEQ:TOK].bitcast(F32), ALU.subtract
                            ).then_inc(S("att_split"), 1)
        with dve.Fori(0, 8) as i:
            for p in range(2):
                j = 2 * i + p
                dve.wait_ge(unit_done[p], Q_F2 + i + 1)
                v.tensor_tensor(halves(big1[:, j, :]), accv[p], halves(big1[:, j, :]), ALU.mult).then_inc(acc_free[p], 1)
                dve.wait_ge(acc_free[p], N_F2 + i + 1)
                v.tensor_tensor(big2[:, j, :], big1[:, j, :], big2[:, j, :], ALU.add).then_inc(S("m_ready"), 1)
        v.memset(sm[:].bitcast(F32), 0.0).then_inc(S("sm_zero"), 1)
        for k in range(KT):
            dve.wait_ge(S("m_hi_ready"), k + 1)
            v.tensor_tensor(act_lo[:, k, :], big2[:, k, :], act_hi[:, k, :].bitcast(F32), ALU.subtract
                            ).then_inc(S("m_split"), 1)
        dve.wait_ge(S("sm_hi_ready"), 1)
        v.tensor_tensor(sm[:, :, NB:2 * NB], big2[:, :, SEQ:TOK], sm[:, :, 0:NB].bitcast(F32), ALU.subtract
                        ).then_inc(S("sm_ready"), 1)
        lo(Q_G, 1)
        lo(Q_G + 1, 1)
        dve.wait_ge(S("g_landed"), 48)
        dve.wait_ge(S("xs2_landed"), 16)

        def chunk(c, last=False):
            dve.wait_ge(S("xch_landed"), 16 * (c + 1))
            for i in range(4):
                y = yrow[:, i, bass.ds(512 * c, 512)]
                dve.wait_ge(S("y_mm"), 5 * c + i + 1)
                v.tensor_tensor(y, ps[:, i, :], gate_p[:, bass.ds(512 * c, 512)], ALU.mult).then_inc(S("y_free"), 1)
                dve.wait_ge(S("y_free"), 5 * c + i + 1)
                v.tensor_tensor(y, y, xch[:, i, :], ALU.add).then_inc(S("y_added"), 1)
            dve.wait_ge(S("y_mm"), 5 * c + 5)
            v.tensor_copy(srow[:], acc[0][0:16, 0, :]).then_inc(S("srow_ready"), 1)
            dve.wait_ge(unit_done[1], Q_G + 2 * c + 2)
            v.tensor_tensor(srow[0:NB, :], acc[0][0:NB, 1, :], gate_s[:, bass.ds(512 * c, 512)], ALU.mult
                            ).then_inc(S("y_free"), 1)
            dve.wait_ge(S("y_free"), 5 * c + 5)
            y = ys[:, bass.ds(512 * c, 512)]
            v.tensor_tensor(y, y, srow[0:NB, :], ALU.add).then_inc(S("ys_added"), 1)

        with dve.Fori(0, 3) as c:
            chunk(c)
            lo(Q_G + 2 * c + 2, 1)
            lo(Q_G + 2 * c + 3, 1)
        chunk(3)
        dve.wait_ge(S("ys_added"), 4)
        dve.wait_ge(S("y_added"), 16)
        v.memset(max8, 0.0).then_inc(S("y_all"), 1)
        for i in range(5):
            n = P if i < 4 else NB
            y = yrow[:, i, :] if i < 4 else ys[:]
            inverse_root(n, i, i + 6)
            v.scalar_tensor_tensor(y, y, rstd[0:n, i:i + 1], gfin[0:n, :], ALU.mult, ALU.mult).then_inc(S("y_ready"), 1)

    @block.tensor
    def _(pe):
        mm = nc.tensor.matmul

        def tile(q, p, fills, kt=KT, hi_=act_hi, lo_=act_lo, parts=None, free=True, between=None):
            if free:
                pe.wait_ge(acc_free[p], fills)
            pe.wait_ge(lo_ready[p], q + 1)
            for k in range(kt):
                if parts is not None:
                    pe.wait_ge(parts, k + 1)
                wh, wl = whi[p][:, k * P:(k + 1) * P], wlo[p][:, k * P:(k + 1) * P]
                for n, (w, x) in enumerate(((wh, hi_), (wh, lo_), (wl, hi_))):
                    for a in range(2):
                        last = mm(acc[p][:, a, 0:HALF], w, x[:, k, a * HALF:(a + 1) * HALF],
                                  start=(k == 0 and n == 0), stop=(k == kt - 1 and n == 2))
                if k == kt - 1:
                    last.then_inc(unit_done[p], 1)
                if between is not None and k % 4 == 3:
                    between(k // 4)

        def cond_chunk(c):
            for u in range(4 * c, 4 * c + 4):
                pe.wait_ge(ring_landed[u % RING], 16 * (u // RING + 1))
                for k in range(4):
                    last = mm(acc[c % 2][0:NB + 1, 0, :], cT[:, 4 * (u % 4) + k, :],
                              ring[u % RING][:, k * 512:(k + 1) * 512],
                              start=(u % 4 == 0 and k == 0), stop=(u % 4 == 3 and k == 3))
                last.then_inc(S("ring_done"), 1)

        tr = nc.tensor.transpose
        pe.wait_ge(S("tables_landed"), 10 * 16)
        tr(ps[:, 0, 0:128], rows_cs[:], ident[:])
        tr(ps[:, 1, 0:16], rows_cp[:], ident[0:16, 0:16])
        tr(ps[:, 1, 16:64], rows_b[:], ident[0:48, 0:48])
        tr(ps[:, 1, 64:88], rows_gs[:], ident[0:24, 0:24]).then_inc(S("rows_T"), 1)
        pe.wait_ge(S("cT_ready"), 1)

        def mod_columns(c):
            pe.wait_ge(S("mod_rows"), c - 3)
            part, g = divmod(ADA_CHUNKS[c], 4)
            if g >= 2:
                pe.wait_ge(S("H_ready"), 4 * g - 7)
            for m in range(4):
                last = tr(modT[g][:, part, m, :], modb[c % 2][:, m * P:(m + 1) * P],
                          ident[0:NB + 1, 0:NB + 1])
            last.then_inc(S("mod_T"), 1)

        for n in range(len(ADA_CHUNKS)):
            if 2 <= n < 6:
                pe.wait_ge(S("gate_rows_ready"), n - 1)
            elif n >= 6:
                pe.wait_ge(S("mod_rows"), n - 5)
            cond_chunk(n)
            if n == 0:
                pe.wait_ge(S("xs_ready"), 1)
                for k in range(KT):
                    last = tr(xsT[:, k, :], xs[:, k * P:(k + 1) * P], ident[0:NB, 0:NB])
                last.then_inc(S("xs_T"), 1)
            if n >= 5:
                mod_columns(n - 1)
            if n in (1, 2, 3, 4):
                i = n - 1
                pe.wait_ge(S("xhat_ready"), i + 1)
                if i:
                    pe.wait_ge(S("xT_act"), i)
                    pe.wait_ge(S("xT_dve"), i)
                for k in range(KT):
                    last = tr(ps[:, k // 4, (k % 4) * P:(k % 4 + 1) * P], x_tok[:, i, k * P:(k + 1) * P], ident[:])
                last.then_inc(S("xT_done"), 1)
        mod_columns(11)
        pe.wait_ge(S("H_ready"), 9)
        tile(Q_A, 0, N_A, parts=S("act_lo_ready"), free=False)
        tile(Q_A, 1, N_A, free=False)

        def score(h, p):
            pe.wait_ge(S("qi_ready"), h + 1)
            pe.wait_ge(S("idx_relu"), h)
            for b in (1, 2, 3):
                last = mm(ps[:, b - 1, 0:(b + 1) * P], qiT[p][:, b * P:(b + 1) * P], kiT[:, 0:(b + 1) * P],
                          start=True, stop=True)
            last.then_inc(S("idx_mm"), 1)

        tile(Q_A + 1, 0, N_A + 1)
        pe.wait_ge(S("ki_ready"), 1)
        for b in (1, 2, 3):
            tr(ps[:, 3, (b - 1) * 16:b * 16], wiT[:, b * P:(b + 1) * P], ident[0:HEADS, 0:HEADS])
        tr(ps[0:NB, 1, 0:P], kiT[:, SEQ:TOK], ident[:])
        for b in range(4):
            last = tr(ps[:, 0, b * P:(b + 1) * P], kiT[:, b * P:(b + 1) * P], ident[:])
        last.then_inc(S("ki_T"), 1)
        tile(Q_A + 1, 1, N_A + 1)
        pe.wait_ge(S("ki_tok_ready"), 1)
        score(0, 0)
        with pe.Fori(1, 8) as i:
            tile(Q_A + 1 + i, 0, N_A + 1 + i)
            score(2 * i - 1, 1)
            tile(Q_A + 1 + i, 1, N_A + 1 + i)
            score(2 * i, 0)

        def kv_transpose(j):
            pe.wait_ge(S("kv_ready"), j + 1)
            if j:
                pe.wait_ge(S("kv_evac"), j)
            src = kT[:, j, :] if j < 4 else vT[j % 2][:]
            for b in range(4):
                last = tr(ps[:, 0, b * P:(b + 1) * P], src[:, b * P:(b + 1) * P], ident[:])
            last.then_inc(S("kv_T"), 1)

        def chunk_transpose(u):
            pe.wait_ge(S(f"kib_landed{u % 3}"), 16 * (u // 3 + 1))
            if u:
                pe.wait_ge(S("si_ka"), u)
            for r in range(4):
                last = tr(ps[:, 2, r * P:(r + 1) * P], kib[u % 3][:, r * P:(r + 1) * P], ident[:])
            last.then_inc(S("si_T"), 1)

        def chunk_score(u):
            pe.wait_ge(S("si_ka"), u + 1)
            if u:
                pe.wait_ge(S("si_relu"), u)
            mm(ps[0:HEADS, 3, :], qiS[:, u % NB, :], kiTc[u % 2][:], start=True, stop=True).then_inc(S("si_qk"), 1)

        def chunk_sum(u):
            n, b = divmod(u, NB)
            pe.wait_ge(S("si_relu"), u + 1)
            if b == 0 and n:
                pe.wait_ge(S("si_q"), n)
            mm(ps[0:NB, 1, :], wiD[:, b, :], reluS[u % 2][:], start=(b == 0), stop=(b == NB - 1)
               ).then_inc(S("si_hr"), 1)

        def chunk_stages(u):
            if u >= 2:
                chunk_sum(u - 2)
            if 1 <= u <= CHUNKS:
                chunk_score(u - 1)
            if u < CHUNKS:
                chunk_transpose(u)

        for j in range(8):
            if j >= 6:
                pe.wait_ge(S("kv_ready"), j - 1)
            tile(Q_B + j // 2, j % 2, N_B + j // 2, free=j < 6,
                 between=(lambda s: chunk_stages(4 * j - 4 + s)) if j else None)
            if j == 0:
                score(15, 1)
                pe.wait_ge(S("idx_relu"), HEADS)
                pe.wait_ge(S("wiD_ready"), 1)
            else:
                kv_transpose(j - 1)
        tile(Q_C, 0, N_C, between=lambda s: chunk_stages(CHUNKS - 4 + s))
        chunk_stages(CHUNKS)
        kv_transpose(7)
        chunk_stages(CHUNKS + 1)
        for b in range(NB):
            if b == 0:
                pe.wait_ge(S("si_relu"), CHUNKS)
            last = mm(ps[0:HEADS, 3, b:b + 1], qiS[:, b, :], kiT[:, SEQ + b:SEQ + b + 1], start=True, stop=True)
        last.then_inc(S("si_qk"), 1)
        pe.wait_ge(S("kv_evac"), 8)
        for kv in range(KVH):
            tr(ps[0:NB, 0, kv * P:(kv + 1) * P], kT[:, kv, SEQ:TOK], ident[:])
        for kv in range(KVH):
            last = tr(ps[0:NB, 2, kv * P:(kv + 1) * P], vS[:, kv, :], ident[:])
        last.then_inc(S("stok_T"), 1)
        pe.wait_ge(S("si_relu"), CHUNKS + 1)
        pe.wait_ge(S("si_q"), 4)
        for b in range(NB):
            last = mm(ps[0:NB, 1, 0:1], wiD[:, b, :], reluS[0][:, b:b + 1], start=(b == 0), stop=(b == NB - 1))
        last.then_inc(S("si_hr"), 1)
        pe.wait_ge(S("stok_ready"), 1)
        pe.wait_ge(S("mask_ready"), 1)
        pe.wait_ge(S("identb_ready"), 1)

        def transpose_prob(hp1):
            pe.wait_ge(S("prob_ready"), hp1)
            for (qb, kb), n in PT_AT.items():
                last = tr(ps[:, n // 4, (n % 4) * P:(n % 4 + 1) * P],
                          prob[:, OFF[qb] + kb * P:OFF[qb] + (kb + 1) * P], ident[:])
            last.then_inc(S("attn_T"), 1)

        def values(hp1):
            pe.wait_ge(S("pt_act"), hp1)
            pe.wait_ge(S("pt_dve"), hp1)
            pe.wait_ge(S("vcur_ready"), hp1)
            for kb in range(4):
                n = PT_AT[kb, kb]
                last = mm(ps[:, 3, kb * P:512], vcur[:, kb, :], probT[:, n * P:(n + 4 - kb) * P],
                          start=(kb == 0), stop=(kb == 3))
            last.then_inc(S("attn_pv"), 1)

        def logits(h):
            pe.wait_ge(S("q_ready"), h + 1)
            for b in range(4):
                bank, c = S_AT[b]
                o = ps[:, bank, c:c + (b + 1) * P]
                mm(o, identb[:], maskb[:, OFF[b]:OFF[b] + (b + 1) * P], start=True, stop=False)
                last = mm(o, qT[:, b * P:(b + 1) * P],
                          kT[:].rearrange("p k n -> p (k n)")[:, bass.ds((h // 4) * TOK, (b + 1) * P)]
                          if not isinstance(h, int) else kT[:, h // 4, 0:(b + 1) * P], start=False, stop=True)
            last.then_inc(S("attn_qk"), 1)

        tile(Q_C, 1, N_C)
        logits(0)
        with pe.Fori(1, HEADS) as h:
            tile(Q_C + h, 0, N_C + h)
            transpose_prob(h)
            tile(Q_C + h, 1, N_C + h)
            values(h)
            logits(h)
        transpose_prob(HEADS)
        values(HEADS)
        for g in range(4):
            q = Q_D + 2 * g
            for p in range(2):
                j = 2 * g + p
                tile(q, p, N_D + 2 * g)
                if j == 0:
                    pe.wait_ge(S("pool_landed"), 32)
                    pe.wait_ge(S("attn_evac"), HEADS)
                if j >= 2:
                    pe.wait_ge(S("u_tok_ready"), j - 1)
                tr(ps[:, p, 0:NB * STATE], state[:, j * P:(j + 1) * P], ident[0:120, 0:120]).then_inc(S("state_T"), 1)
                pe.wait_ge(S("u_ready"), j + 1)
                tr(ps[0:STATE, p, 128:256], ub[p][:, 16 + SEQ - STATE:16 + SEQ], ident[:])
                tr(ps[0:NB, p, 256:384], ext[p][:, :, 15], ident[:]).then_inc(S("u_T"), 1)
            for p in range(2):
                j = 2 * g + p
                tile(q + 1, p, N_D + 2 * g + 1)
                pe.wait_ge(S("pooled_ready"), 2 * g + 2)
                if j:
                    pe.wait_ge(S("pg_ready"), j)
                for a in range(2):
                    for c in range(2):
                        last = mm(ps[:, 2 + a, 0:HALF], wpool[:, g, c, p * P:(p + 1) * P],
                                  pooled[:, c, a * HALF:(a + 1) * HALF], start=(c == 0), stop=(c == 1))
                last.then_inc(S("mix_mm"), 1)
        pe.wait_ge(S("pool_ready"), 8)
        with pe.Fori(0, KT) as j:
            tile(Q_E + j, 0, N_E + j)
            tile(Q_E + j, 1, N_E + j, kt=8, hi_=pool_hi, lo_=pool_lo)
        pe.wait_ge(S("rowf_ready"), 1)
        for hf in range(2):
            last = tr(ps[:, 3, hf * NB:(hf + 1) * NB], rowf[:, 5, hf * P:(hf + 1) * P], ident[0:NB, 0:NB])
        last.then_inc(S("rowf_T"), 1)
        for b in range(NB):
            pe.wait_ge(S("sa_sel"), 64 * (b + 1))
            for kv in range(KVH):
                for hf in range(2):
                    last = tr(ps[:, kv // 2, (kv % 2) * 256 + hf * P:(kv % 2) * 256 + (hf + 1) * P],
                              ksel[:, hf, kv * P:(kv + 1) * P], ident[:])
            last.then_inc(S("sa_T"), 1)
            pe.wait_ge(S("sa_ka"), b + 1)
            pe.wait_ge(S("sa_kd"), b + 1)
            for kv in range(KVH):
                last = mm(ps[0:HEADS, 2, 0:256], qSm[:, b, kv, :], kselT[:, kv, :], start=(kv == 0), stop=(kv == 3))
            last.then_inc(S("sa_qk"), 1)
            pe.wait_ge(S("sa_prob"), b + 1)
            for hf in range(2):
                last = tr(ps[:, 2, 256 + hf * HEADS:256 + (hf + 1) * HEADS], pS[:, hf * P:(hf + 1) * P],
                          ident[0:HEADS, 0:HEADS])
            last.then_inc(S("sa_pT"), 1)
            pe.wait_ge(S("sa_pst"), b + 1)
            if b:
                pe.wait_ge(S("attS_ready"), b)
            else:
                pe.wait_ge(S("rows_ready"), 1)
            for kv in range(KVH):
                for hf in range(2):
                    last = mm(ps[:, 3, 64 + 4 * kv:68 + 4 * kv], vsel[:, hf, kv * P:(kv + 1) * P],
                              pST[:, hf, 4 * kv:4 * kv + 4], start=(hf == 0), stop=(hf == 1))
            last.then_inc(S("sa_pv"), 1)
        with pe.Fori(0, 8) as i:
            tile(Q_F1 + i, 0, N_F1 + i)
            tile(Q_F1 + i, 1, N_F1 + i)
        tile(Q_F2, 0, N_F2, parts=S("att_split"))
        tile(Q_F2, 1, N_F2)
        with pe.Fori(1, 8) as i:
            tile(Q_F2 + i, 0, N_F2 + i)
            tile(Q_F2 + i, 1, N_F2 + i)

        def out_chunk(c, first=False):
            for kq in range(4):
                q, p = Q_G + 2 * c + kq // 2, kq % 2
                pe.wait_ge(lo_ready[p], q + 1)
                for i in range(5):
                    if kq == 0:
                        if not first:
                            pe.wait_ge(S("y_free"), 5 * c - 4 + i)
                        elif i in (0, 4):
                            pe.wait_ge(acc_free[0], N_G)
                            pe.wait_ge(S("attS_ready"), NB)
                    for kk in range(4):
                        k = 4 * kq + kk
                        if first and i == 0:
                            pe.wait_ge(S("m_split"), k + 1)
                        if first and i == 4 and k == 0:
                            pe.wait_ge(S("sm_ready"), 1)
                        wh, wl = (w[p][:, kk * 512:(kk + 1) * 512] for w in (whi, wlo))
                        if i < 4:
                            s = slice(i * P, (i + 1) * P)
                            trio = ((act_hi[:, k, s], wh), (act_hi[:, k, s], wl), (act_lo[:, k, s], wh))
                            o = ps[:, i, :]
                        else:
                            trio = ((sm[:, k, :], wh), (sm[:, k, :], wl))
                            o = acc[0][:, 0, :]
                        for n, (x, w) in enumerate(trio):
                            last = mm(o, x, w, start=(k == 0 and n == 0), stop=(k == KT - 1 and n == len(trio) - 1))
                    if kq == 3 and i < 4:
                        last.then_inc(S("y_mm"), 1)
                if kq < 3:
                    last.then_inc(unit_done[p], 1)
            last.then_inc(S("y_mm"), 1)
            pe.wait_ge(S("srow_ready"), c + 1)
            mm(acc[0][0:64, 1, :], sel8, srow[:], start=True, stop=True).then_inc(unit_done[1], 1)

        out_chunk(0, first=True)
        with pe.Fori(1, 4) as c:
            out_chunk(c)

    ctx.close()


_INS = ['x_prompt', 'x_sample', 'c_prompt', 'c_sample', 'cache_k', 'cache_v', 'cache_kidx', 'state_pool', 'page_table',
        'g_norm', 'w_ada', 'b_ada', 'w_in', 'w_pool', 's_pool', 'w_a_proj', 'w_b_proj', 'w_out', 'g_final']
_OUTS = [('y_p', (SEQ, D), (1, SEQ, D)), ('y_s', (NB, D), (NB, 1, D)),
         ('k_p', (SEQ, 512), (1, 1, SEQ, KVH, P)), ('v_p', (SEQ, 512), (1, 1, SEQ, KVH, P)),
         ('kidx_p', (SEQ, P), (1, 1, SEQ, P)), ('pool_p', (STATE, PW), (1, 1, STATE, PW)),
         ('k_s', (NB, 512), (1, NB, 1, KVH, P)), ('v_s', (NB, 512), (1, NB, 1, KVH, P)),
         ('kidx_s', (NB, P), (1, NB, 1, P)), ('pool_s', (NB, STATE, PW), (1, NB, STATE, PW))]


def shape_constants():
    pos = np.concatenate([np.arange(SEQ), np.full(NB, PAST)]).astype(np.float32)
    inv = np.float32(10000.0) ** (-np.arange(64, dtype=np.float32) / np.float32(64))
    ang = pos[None, :] * inv[:, None]
    cos, sin = np.cos(ang).astype(np.float32), np.sin(ang).astype(np.float32)
    sel = np.zeros((16, 64), np.float32)
    for r in range(16):
        sel[r, r % 8] = 1.0
    cnt = np.stack([np.minimum(np.arange(16) + 1, w) for w in WINDOWS]).astype(np.float32)
    return {
        "k_cos": np.concatenate([cos, cos]), "k_sin": np.concatenate([sin, -sin]),
        "k_ident": np.eye(P, dtype=np.float32), "k_sel": sel,
        "k_rcnt": np.ascontiguousarray(np.broadcast_to((1.0 / cnt).astype(np.float32).reshape(1, 64), (P, 64))),
        "k_lane": (np.arange(P) % 32).astype(np.float32).reshape(P, 1),
        "k_tri": np.where(np.arange(P)[None, :] > np.arange(P)[:, None], np.float32(MASKED), np.float32(0.0)),
    }


def kernel(**inputs):
    from concourse import bacc
    from concourse.bass_utils import run_bass_kernel_spmd

    nc = bacc.Bacc("TRN2", target_bir_lowering=False, num_devices=1)
    arrays = {n: np.ascontiguousarray(inputs[n]) for n in _INS}
    arrays.update(shape_constants())
    t = {n: nc.dram_tensor("in_" + n, a.shape, mybir.dt.from_np(a.dtype), kind="ExternalInput").ap()
         for n, a in arrays.items()}
    t["n_pool"] = arrays["cache_k"].shape[1]
    out = {n: nc.dram_tensor("out_" + n, shape, F32, kind="ExternalOutput").ap() for n, shape, _ in _OUTS}
    build(nc, t, out)
    r = run_bass_kernel_spmd(nc, [{"in_" + n: a for n, a in arrays.items()}], core_ids=[0])
    return tuple(r.results[0]["out_" + n].reshape(full) for n, _, full in _OUTS)
```
